# Optimizing a Trainium2 kernel written in Bass

```python
import jax
import jax.numpy as jnp
from jax import lax
import numpy as np
import jax, jax.numpy as jnp

D_MODEL = 1024
BATCH = 1
SEQ = 512
DEPTH = 2

HEAD_DIM = 64
N_HEADS = D_MODEL // HEAD_DIM
SB_HEADS = N_HEADS // 2
NSA_HEADS = N_HEADS - SB_HEADS
NSA_KV_GROUPS = 2
FOX_HEADS = N_HEADS
CMP_LEN = 32
CMP_STRIDE = 16
SEL_LEN = 64
SEL_TOP = 16
WINDOW = 512
N_BRANCH = 3
Q_BLOCK = 128
ROPE_THETA = 500000.0
ROT_DIM = HEAD_DIM // 4
D_FF = 256 * ((8 * D_MODEL // 3 + 255) // 256)
CONV_WIDTH = 3
NORM_EPS = 1e-6
N_EVEN = (DEPTH + 1) // 2
N_ODD = DEPTH // 2
SB_W = SB_HEADS * HEAD_DIM
NSA_QW = NSA_HEADS * HEAD_DIM
NSA_KVW = NSA_KV_GROUPS * HEAD_DIM
EVEN_SPLITS = (SB_W, SB_W, SB_W, NSA_QW) + (NSA_KVW,) * 6 + (NSA_HEADS * N_BRANCH,)
EVEN_IN = sum(EVEN_SPLITS)
FOX_W = FOX_HEADS * HEAD_DIM
ODD_SPLITS = (FOX_W, FOX_W, FOX_W, FOX_HEADS)
ODD_IN = sum(ODD_SPLITS)


def rmsnorm(x, g):
    x32 = x.astype(jnp.float32)
    y = x32 * lax.rsqrt(jnp.mean(x32 * x32, axis=-1, keepdims=True) + NORM_EPS)
    return y.astype(x.dtype) * g

def split_cols(h, sizes):
    offs = np.cumsum(sizes)[:-1].tolist()
    return jnp.split(h, offs, axis=-1)

def partial_rope(x, pos):
    half = ROT_DIM // 2
    inv_freq = ROPE_THETA ** (-(jnp.arange(half, dtype=jnp.float32) * 2.0 / ROT_DIM))
    ang = pos[:, None] * inv_freq[None, :]
    cos = jnp.cos(ang)[None, :, None, :].astype(x.dtype)
    sin = jnp.sin(ang)[None, :, None, :].astype(x.dtype)
    x1 = x[..., :half]
    x2 = x[..., half:ROT_DIM]
    return jnp.concatenate([x1 * cos - x2 * sin, x1 * sin + x2 * cos, x[..., ROT_DIM:]], axis=-1)

def masked_softmax(s, mask):
    s = jnp.where(mask, s, -jnp.inf)
    m = jnp.max(s, axis=-1, keepdims=True)
    m = jnp.where(jnp.isfinite(m), m, 0.0)
    e = jnp.where(mask, jnp.exp(s - m), 0.0)
    d = jnp.sum(e, axis=-1, keepdims=True)
    return e / jnp.where(d > 0, d, 1.0)

def sweep_query_blocks(fn, seq):
    out = lax.map(fn, jnp.arange(seq // Q_BLOCK))
    nb, bsz, q, nh, dh = out.shape
    return jnp.moveaxis(out, 0, 1).reshape(bsz, nb * q, nh, dh)

def stick_breaking_attention(q, k, v):
    bsz, seq, nh, dh = q.shape
    scale = dh ** -0.5
    kpos = jnp.arange(seq)

    def block(i):
        q0 = i * Q_BLOCK
        qb = lax.dynamic_slice_in_dim(q, q0, Q_BLOCK, axis=1)
        tpos = q0 + jnp.arange(Q_BLOCK)
        z = jnp.einsum('bqhd,bshd->bhqs', qb, k, preferred_element_type=jnp.float32) * scale
        mask = kpos[None, :] < tpos[:, None]
        log_keep = jnp.where(mask, jax.nn.log_sigmoid(-z), 0.0)
        after = lax.cumsum(log_keep, axis=3, reverse=True) - log_keep
        a = jnp.where(mask, jnp.exp(jax.nn.log_sigmoid(z) + after), 0.0)
        return jnp.einsum('bhqs,bshd->bqhd', a.astype(v.dtype), v)

    return sweep_query_blocks(block, seq)

def forgetting_attention(q, k, v, log_f):
    bsz, seq, nh, dh = q.shape
    scale = dh ** -0.5
    kpos = jnp.arange(seq)
    cum = jnp.transpose(jnp.cumsum(log_f, axis=1), (0, 2, 1))

    def block(i):
        q0 = i * Q_BLOCK
        qb = lax.dynamic_slice_in_dim(q, q0, Q_BLOCK, axis=1)
        cq = lax.dynamic_slice_in_dim(cum, q0, Q_BLOCK, axis=2)
        tpos = q0 + jnp.arange(Q_BLOCK)
        s = jnp.einsum('bqhd,bshd->bhqs', qb, k, preferred_element_type=jnp.float32) * scale
        s = s + (cq[..., :, None] - cum[..., None, :])
        p = masked_softmax(s, kpos[None, :] <= tpos[:, None])
        return jnp.einsum('bhqs,bshd->bqhd', p.astype(v.dtype), v)

    return sweep_query_blocks(block, seq)

def nsa_attention(q, k_cmp, v_cmp, k_slc, v_slc, k_win, v_win, gates, pos_k, pos_v, w_ck, w_cv):
    bsz, seq, nh, dh = q.shape
    ng = k_cmp.shape[2]
    rep = nh // ng
    scale = dh ** -0.5
    n_cmp = (seq - CMP_LEN) // CMP_STRIDE + 1
    c_start = jnp.arange(n_cmp) * CMP_STRIDE
    cidx = c_start[:, None] + jnp.arange(CMP_LEN)[None, :]

    def compress(t, pe, w):
        blocks = t[:, cidx] + pe[None, None, :, None, :]
        blocks = jnp.moveaxis(blocks, 3, 2).reshape(bsz, n_cmp, ng, CMP_LEN * dh)
        return blocks @ w

    cmp_end = c_start + CMP_LEN - 1
    kc = partial_rope(compress(k_cmp, pos_k, w_ck), cmp_end.astype(jnp.float32))
    vc = compress(v_cmp, pos_v, w_cv)
    n_sel = seq // SEL_LEN
    top = min(SEL_TOP, n_sel)
    ks = k_slc.reshape(bsz, n_sel, SEL_LEN, ng, dh).transpose(0, 3, 1, 2, 4)
    vs = v_slc.reshape(bsz, n_sel, SEL_LEN, ng, dh).transpose(0, 3, 1, 2, 4)
    sel_start = jnp.arange(n_sel) * SEL_LEN
    overlap = (c_start[:, None] < sel_start[None, :] + SEL_LEN) & (c_start[:, None] + CMP_LEN > sel_start[None, :])
    cmp_to_sel = overlap.astype(jnp.float32)
    blk = jnp.arange(n_sel)
    bi = jnp.arange(bsz)[:, None, None, None]
    gi = jnp.arange(ng)[None, :, None, None]
    kw = jnp.pad(k_win, ((0, 0), (WINDOW, 0), (0, 0), (0, 0)))
    vw = jnp.pad(v_win, ((0, 0), (WINDOW, 0), (0, 0), (0, 0)))

    def block(i):
        q0 = i * Q_BLOCK
        tpos = q0 + jnp.arange(Q_BLOCK)
        qb = lax.dynamic_slice_in_dim(q, q0, Q_BLOCK, axis=1).reshape(bsz, Q_BLOCK, ng, rep, dh)
        sc = jnp.einsum('bqgrd,bcgd->bgrqc', qb, kc, preferred_element_type=jnp.float32) * scale
        pc = masked_softmax(sc, cmp_end[None, :] <= tpos[:, None])
        o_cmp = jnp.einsum('bgrqc,bcgd->bqgrd', pc.astype(vc.dtype), vc)
        imp = jnp.einsum('bgrqc,cn->bgqn', pc, cmp_to_sel)
        cur = tpos // SEL_LEN
        causal = blk[None, :] <= cur[:, None]
        forced = (blk[None, :] == 0) | (blk[None, :] == cur[:, None]) | (blk[None, :] == cur[:, None] - 1)
        score = jnp.where(causal, jnp.where(forced, jnp.inf, imp), -jnp.inf)
        top_val, top_idx = lax.top_k(score, top)
        sel_ok = top_val > -jnp.inf
        kg = ks[bi, gi, top_idx]
        vg = vs[bi, gi, top_idx]
        kpos = top_idx[..., None] * SEL_LEN + jnp.arange(SEL_LEN)
        smask = sel_ok[..., None] & (kpos <= tpos[None, None, :, None, None])
        ss = jnp.einsum('bqgrd,bgqnld->bgrqnl', qb, kg, preferred_element_type=jnp.float32) * scale
        ps = masked_softmax(ss.reshape(bsz, ng, rep, Q_BLOCK, top * SEL_LEN),
                            smask.reshape(bsz, ng, 1, Q_BLOCK, top * SEL_LEN))
        ps = ps.reshape(bsz, ng, rep, Q_BLOCK, top, SEL_LEN)
        o_slc = jnp.einsum('bgrqnl,bgqnld->bqgrd', ps.astype(vg.dtype), vg)
        kwb = lax.dynamic_slice_in_dim(kw, q0, Q_BLOCK + WINDOW, axis=1)
        vwb = lax.dynamic_slice_in_dim(vw, q0, Q_BLOCK + WINDOW, axis=1)
        wpos = q0 - WINDOW + jnp.arange(Q_BLOCK + WINDOW)
        wmask = (wpos[None, :] >= 0) & (wpos[None, :] <= tpos[:, None]) & (wpos[None, :] > tpos[:, None] - WINDOW)
        sw = jnp.einsum('bqgrd,bkgd->bgrqk', qb, kwb, preferred_element_type=jnp.float32) * scale
        pw = masked_softmax(sw, wmask)
        o_win = jnp.einsum('bgrqk,bkgd->bqgrd', pw.astype(vwb.dtype), vwb)
        gb = lax.dynamic_slice_in_dim(gates, q0, Q_BLOCK, axis=1).reshape(bsz, Q_BLOCK, ng, rep, N_BRANCH)
        o = gb[..., 0:1] * o_cmp + gb[..., 1:2] * o_slc + gb[..., 2:3] * o_win
        return o.reshape(bsz, Q_BLOCK, nh, dh)

    return sweep_query_blocks(block, seq)

def even_mixer(h, w_in, pos_k, pos_v, w_ck, w_cv, w_out):
    bsz, seq, _ = h.shape
    sq, sk, sv, nq, kc, vc, ksl, vsl, kwn, vwn, g = split_cols(h @ w_in, EVEN_SPLITS)
    pos = jnp.arange(seq, dtype=jnp.float32)

    def heads(t):
        return t.reshape(bsz, seq, -1, HEAD_DIM)

    o_sb = stick_breaking_attention(heads(sq), heads(sk), heads(sv))
    o_nsa = nsa_attention(partial_rope(heads(nq), pos), heads(kc), heads(vc),
                          partial_rope(heads(ksl), pos), heads(vsl),
                          partial_rope(heads(kwn), pos), heads(vwn),
                          jax.nn.sigmoid(g.reshape(bsz, seq, NSA_HEADS, N_BRANCH)),
                          pos_k, pos_v, w_ck, w_cv)
    o = jnp.concatenate([o_sb.reshape(bsz, seq, SB_W), o_nsa.reshape(bsz, seq, NSA_QW)], axis=-1)
    return o @ w_out

def odd_mixer(h, w_in, b_f, w_out):
    bsz, seq, _ = h.shape
    q, k, v, f = split_cols(h @ w_in, ODD_SPLITS)
    log_f = jax.nn.log_sigmoid((f + b_f).astype(jnp.float32))
    o = forgetting_attention(q.reshape(bsz, seq, FOX_HEADS, HEAD_DIM),
                             k.reshape(bsz, seq, FOX_HEADS, HEAD_DIM),
                             v.reshape(bsz, seq, FOX_HEADS, HEAD_DIM), log_f)
    return o.reshape(bsz, seq, FOX_W) @ w_out

def conv_glu_ffn(h, w_in, conv_w, conv_b, w_out):
    a, b = jnp.split(h @ w_in, 2, axis=-1)
    taps = conv_w[:, None, :]
    a = lax.conv_general_dilated(a, taps, window_strides=(1,), padding=[(CONV_WIDTH - 1, 0)],
                                 dimension_numbers=('NWC', 'WIO', 'NWC'),
                                 feature_group_count=a.shape[-1]) + conv_b
    return (jax.nn.silu(a) * b) @ w_out

def first_inputs(seed: int = 0) -> dict:
    key = jax.random.key(seed)
    k = jax.random.split(key, 17)

    def nrm(kk, shape, scale):
        return jax.random.normal(kk, shape, jnp.float32) * scale

    d = D_MODEL
    lc = CMP_LEN * HEAD_DIM
    return {
        'x': nrm(k[0], (BATCH, SEQ, d), 1.0),
        'attn_norm': 1.0 + nrm(k[1], (DEPTH, d), 0.02),
        'ffn_norm': 1.0 + nrm(k[2], (DEPTH, d), 0.02),
        'ev_w_in': nrm(k[3], (N_EVEN, d, EVEN_IN), d ** -0.5),
        'ev_cmp_pos_k': nrm(k[4], (N_EVEN, CMP_LEN, HEAD_DIM), 0.2),
        'ev_cmp_pos_v': nrm(k[5], (N_EVEN, CMP_LEN, HEAD_DIM), 0.2),
        'ev_cmp_w_k': nrm(k[6], (N_EVEN, lc, HEAD_DIM), lc ** -0.5),
        'ev_cmp_w_v': nrm(k[7], (N_EVEN, lc, HEAD_DIM), lc ** -0.5),
        'ev_w_out': nrm(k[8], (N_EVEN, SB_W + NSA_QW, d), (SB_W + NSA_QW) ** -0.5),
        'od_w_in': nrm(k[9], (N_ODD, d, ODD_IN), d ** -0.5),
        'od_b_f': 2.0 + nrm(k[10], (N_ODD, FOX_HEADS), 0.5),
        'od_w_out': nrm(k[11], (N_ODD, FOX_W, d), FOX_W ** -0.5),
        'ffn_w_in': nrm(k[12], (DEPTH, d, 2 * D_FF), d ** -0.5),
        'ffn_conv_w': nrm(k[13], (DEPTH, CONV_WIDTH, D_FF), CONV_WIDTH ** -0.5),
        'ffn_conv_b': nrm(k[14], (DEPTH, D_FF), 0.02),
        'ffn_w_out': nrm(k[15], (DEPTH, D_FF, d), D_FF ** -0.5),
        'final_norm': 1.0 + nrm(k[16], (d,), 0.02),
    }

def first_block(x, attn_norm, ffn_norm, ev_w_in, ev_cmp_pos_k, ev_cmp_pos_v, ev_cmp_w_k, ev_cmp_w_v,
              ev_w_out, od_w_in, od_b_f, od_w_out, ffn_w_in, ffn_conv_w, ffn_conv_b, ffn_w_out,
              final_norm):
    for layer in range(DEPTH):
        h = rmsnorm(x, attn_norm[layer])
        if layer % 2 == 0:
            e = layer // 2
            x = x + even_mixer(h, ev_w_in[e], ev_cmp_pos_k[e], ev_cmp_pos_v[e],
                               ev_cmp_w_k[e], ev_cmp_w_v[e], ev_w_out[e])
        else:
            o = layer // 2
            x = x + odd_mixer(h, od_w_in[o], od_b_f[o], od_w_out[o])
        x = x + conv_glu_ffn(rmsnorm(x, ffn_norm[layer]), ffn_w_in[layer], ffn_conv_w[layer],
                             ffn_conv_b[layer], ffn_w_out[layer])
    return rmsnorm(x, final_norm)


DEPTH_2 = 1

CTX_LEN = 256
GRID_W = 64
NA_HEADS = 8
NA_WIDTH = NA_HEADS * HEAD_DIM
NA_WIN_ROWS = 8
NA_WIN_COLS = 16
GM_GROUPS = 8
GM_CHUNK = 128
GM_WIDTH = D_MODEL // 2
GM_GROUP_DIM = GM_WIDTH // GM_GROUPS
PEER_HEADS = 8
PEER_N_KEYS = 128
PEER_EXPERTS = PEER_N_KEYS * PEER_N_KEYS
PEER_TOPK = 16
PEER_QDIM = 256
PEER_HALF = PEER_QDIM // 2
PEER_BLOCK = 128
ADA_CHUNKS = 6
EPS = 1e-6
NEG_INF = -1e30
IN_SPLITS = (NA_WIDTH, 2 * NA_WIDTH, 3 * NA_WIDTH, 3 * NA_WIDTH + GM_WIDTH,
             3 * NA_WIDTH + 2 * GM_WIDTH, 3 * NA_WIDTH + 2 * GM_WIDTH + D_MODEL)
IN_COLS = 3 * NA_WIDTH + 2 * GM_WIDTH + 2 * D_MODEL


def rmsnorm_2(x, g):
    xf = x.astype(jnp.float32)
    y = xf * lax.rsqrt(jnp.mean(xf * xf, axis=-1, keepdims=True) + EPS)
    return (y * g.astype(jnp.float32)).astype(x.dtype)

def layernorm(x, g):
    xf = x.astype(jnp.float32)
    xc = xf - jnp.mean(xf, axis=-1, keepdims=True)
    y = xc * lax.rsqrt(jnp.mean(xc * xc, axis=-1, keepdims=True) + EPS)
    return (y * g.astype(jnp.float32)).astype(x.dtype)

def modulate(h, shift, scale):
    return h * (1 + scale) + shift

def heads(z):
    return z.reshape(z.shape[:-1] + (NA_HEADS, HEAD_DIM))

def neighborhood_attention(q, k, v, k_ctx, v_ctx, rpb):
    B, S = q.shape[0], q.shape[1]
    rows = S // GRID_W
    kh = min(NA_WIN_ROWS, rows)
    band = kh * GRID_W
    scale = HEAD_DIM ** -0.5
    qg = q.reshape(B, rows, GRID_W, NA_HEADS, HEAD_DIM)
    kg = k.reshape(B, rows, GRID_W, NA_HEADS, HEAD_DIM)
    vg = v.reshape(B, rows, GRID_W, NA_HEADS, HEAD_DIM)
    col = jnp.arange(GRID_W)
    col_start = jnp.clip(col - NA_WIN_COLS // 2, 0, GRID_W - NA_WIN_COLS)
    col_in = (col[None, :] >= col_start[:, None]) & (col[None, :] < col_start[:, None] + NA_WIN_COLS)
    band_mask = jnp.broadcast_to(col_in[:, None, :], (GRID_W, kh, GRID_W)).reshape(GRID_W, band)
    dc_idx = jnp.clip(col[None, :] - col[:, None] + NA_WIN_COLS - 1, 0, 2 * NA_WIN_COLS - 2)

    def row_step(r):
        rs = jnp.clip(r - NA_WIN_ROWS // 2, 0, rows - kh)
        q_r = lax.dynamic_index_in_dim(qg, r, axis=1, keepdims=False)
        k_b = lax.dynamic_slice_in_dim(kg, rs, kh, axis=1).reshape(B, band, NA_HEADS, HEAD_DIM)
        v_b = lax.dynamic_slice_in_dim(vg, rs, kh, axis=1).reshape(B, band, NA_HEADS, HEAD_DIM)
        dr_idx = rs + jnp.arange(kh) - r + NA_WIN_ROWS - 1
        bias = rpb[:, dr_idx][:, :, dc_idx]
        bias = bias.transpose(0, 2, 1, 3).reshape(NA_HEADS, GRID_W, band).astype(jnp.float32)
        s_loc = jnp.einsum('bqhd,bkhd->bhqk', q_r, k_b).astype(jnp.float32) * scale + bias
        s_loc = jnp.where(band_mask, s_loc, NEG_INF)
        s_ctx = jnp.einsum('bqhd,bchd->bhqc', q_r, k_ctx).astype(jnp.float32) * scale
        p = jax.nn.softmax(jnp.concatenate([s_loc, s_ctx], axis=-1), axis=-1).astype(v.dtype)
        return (jnp.einsum('bhqk,bkhd->bqhd', p[..., :band], v_b)
                + jnp.einsum('bhqc,bchd->bqhd', p[..., band:], v_ctx))

    o = lax.map(row_step, jnp.arange(rows))
    return jnp.moveaxis(o, 0, 1).reshape(B, S, NA_WIDTH)

def context_attention(q, k, v):
    s = jnp.einsum('bqhd,bkhd->bhqk', q, k).astype(jnp.float32) * (HEAD_DIM ** -0.5)
    p = jax.nn.softmax(s, axis=-1).astype(v.dtype)
    o = jnp.einsum('bhqk,bkhd->bqhd', p, v)
    return o.reshape(o.shape[0], o.shape[1], NA_WIDTH)

def spatial_gating(gu, gv, ln_g, ws, bs):
    B, L, _ = gv.shape
    n = L // GM_CHUNK
    u = jax.nn.gelu(gu)
    vn = layernorm(jax.nn.gelu(gv), ln_g)
    vg = vn.reshape(B, n, GM_CHUNK, GM_GROUPS, GM_GROUP_DIM)
    mixed = jnp.einsum('gpq,bnqgd->bnpgd', ws, vg) + bs.T[:, :, None]
    return u * mixed.reshape(B, L, GM_WIDTH)

def merge_branches(y_a, y_b, ga, gb, w_pa, w_pb, w_out):
    m = jax.nn.sigmoid(ga) * (y_a @ w_pa) + jax.nn.sigmoid(gb) * (y_b @ w_pb)
    return m @ w_out

def peer_ffn(h, wq, sub_keys, expert_u, expert_v):
    B, L, D = h.shape
    blocks = h.reshape(B * L // PEER_BLOCK, PEER_BLOCK, D)

    def block(xb):
        q = (xb @ wq).reshape(PEER_BLOCK, PEER_HEADS, 2, PEER_HALF)
        s = jnp.einsum('thpd,hpkd->thpk', q, sub_keys).astype(jnp.float32)
        s_top, i_top = lax.top_k(s, PEER_TOPK)
        cand_s = (s_top[:, :, 0, :, None] + s_top[:, :, 1, None, :]).reshape(PEER_BLOCK, PEER_HEADS, PEER_TOPK * PEER_TOPK)
        cand_i = (i_top[:, :, 0, :, None] * PEER_N_KEYS + i_top[:, :, 1, None, :]).reshape(PEER_BLOCK, PEER_HEADS, PEER_TOPK * PEER_TOPK)
        best_s, best_pos = lax.top_k(cand_s, PEER_TOPK)
        experts = jnp.take_along_axis(cand_i, best_pos, axis=-1)
        g = jax.nn.softmax(best_s, axis=-1)
        act = jax.nn.gelu(jnp.einsum('thkd,td->thk', expert_u[experts], xb).astype(jnp.float32))
        wgt = (g * act).astype(xb.dtype)
        return jnp.einsum('thk,thkd->td', wgt, expert_v[experts])

    return lax.map(block, blocks).reshape(B, L, D)

def second_inputs(seed: int = 0) -> dict:
    key = jax.random.key(seed)
    ks = jax.random.split(key, 21)
    nrm = jax.random.normal
    return {
        'x': nrm(ks[0], (BATCH, SEQ, D_MODEL), jnp.float32),
        'c': nrm(ks[1], (BATCH, D_MODEL), jnp.float32),
        'ctx': nrm(ks[2], (BATCH, CTX_LEN, D_MODEL), jnp.float32),
        'c_ctx': nrm(ks[3], (D_MODEL,), jnp.float32),
        'ada_w': nrm(ks[4], (DEPTH_2, D_MODEL, ADA_CHUNKS * D_MODEL), jnp.float32) * (0.3 * D_MODEL ** -0.5),
        'ada_b': nrm(ks[5], (DEPTH_2, ADA_CHUNKS * D_MODEL), jnp.float32) * 0.02,
        'norm1_g': 1.0 + 0.01 * nrm(ks[6], (DEPTH_2, D_MODEL), jnp.float32),
        'norm2_g': 1.0 + 0.01 * nrm(ks[7], (DEPTH_2, D_MODEL), jnp.float32),
        'w_in': nrm(ks[8], (DEPTH_2, D_MODEL, IN_COLS), jnp.float32) * D_MODEL ** -0.5,
        'na_rpb': nrm(ks[9], (DEPTH_2, NA_HEADS, 2 * NA_WIN_ROWS - 1, 2 * NA_WIN_COLS - 1), jnp.float32) * 0.1,
        'gm_ln_g': 1.0 + 0.01 * nrm(ks[10], (DEPTH_2, GM_WIDTH), jnp.float32),
        'gm_ws': nrm(ks[11], (DEPTH_2, GM_GROUPS, GM_CHUNK, GM_CHUNK), jnp.float32) * GM_CHUNK ** -0.5,
        'gm_bs': 1.0 + 0.02 * nrm(ks[12], (DEPTH_2, GM_GROUPS, GM_CHUNK), jnp.float32),
        'w_proj_a': nrm(ks[13], (DEPTH_2, NA_WIDTH, D_MODEL), jnp.float32) * NA_WIDTH ** -0.5,
        'w_proj_b': nrm(ks[14], (DEPTH_2, GM_WIDTH, D_MODEL), jnp.float32) * GM_WIDTH ** -0.5,
        'w_out': nrm(ks[15], (DEPTH_2, D_MODEL, D_MODEL), jnp.float32) * D_MODEL ** -0.5,
        'peer_wq': nrm(ks[16], (DEPTH_2, D_MODEL, PEER_HEADS * PEER_QDIM), jnp.float32) * D_MODEL ** -0.5,
        'peer_keys': nrm(ks[17], (DEPTH_2, PEER_HEADS, 2, PEER_N_KEYS, PEER_HALF), jnp.float32) * PEER_HALF ** -0.5,
        'peer_u': nrm(ks[18], (DEPTH_2, PEER_EXPERTS, D_MODEL), jnp.float32) * D_MODEL ** -0.5,
        'peer_v': nrm(ks[19], (DEPTH_2, PEER_EXPERTS, D_MODEL), jnp.float32) * 0.5,
        'final_g': 1.0 + 0.01 * nrm(ks[20], (D_MODEL,), jnp.float32),
    }

def second_block(x, c, ctx, c_ctx, ada_w, ada_b, norm1_g, norm2_g, w_in, na_rpb, gm_ln_g, gm_ws, gm_bs,
              w_proj_a, w_proj_b, w_out, peer_wq, peer_keys, peer_u, peer_v, final_g):
    for layer in range(DEPTH_2):
        last = layer == DEPTH_2 - 1
        sh1, sc1, g1, sh2, sc2, g2 = jnp.split(
            (jax.nn.silu(c) @ ada_w[layer] + ada_b[layer])[:, None, :], ADA_CHUNKS, axis=-1)
        csh1, csc1, cg1, csh2, csc2, cg2 = jnp.split(
            jax.nn.silu(c_ctx) @ ada_w[layer] + ada_b[layer], ADA_CHUNKS, axis=-1)
        w = w_in[layer]
        h = modulate(rmsnorm_2(x, norm1_g[layer]), sh1, sc1)
        hc = modulate(rmsnorm_2(ctx, norm1_g[layer]), csh1, csc1)
        q, k, v, gu, gv, ga, gb = jnp.split(h @ w, IN_SPLITS, axis=-1)
        if last:
            k_c, v_c = jnp.split(hc @ w[:, NA_WIDTH:3 * NA_WIDTH], 2, axis=-1)
        else:
            qc, k_c, v_c, guc, gvc, gac, gbc = jnp.split(hc @ w, IN_SPLITS, axis=-1)
        y_a = neighborhood_attention(heads(q), heads(k), heads(v), heads(k_c), heads(v_c), na_rpb[layer])
        y_b = spatial_gating(gu, gv, gm_ln_g[layer], gm_ws[layer], gm_bs[layer])
        x = x + g1 * merge_branches(y_a, y_b, ga, gb, w_proj_a[layer], w_proj_b[layer], w_out[layer])
        h2 = modulate(rmsnorm_2(x, norm2_g[layer]), sh2, sc2)
        x = x + g2 * peer_ffn(h2, peer_wq[layer], peer_keys[layer], peer_u[layer], peer_v[layer])
        if not last:
            yc_a = context_attention(heads(qc), heads(k_c), heads(v_c))
            yc_b = spatial_gating(guc, gvc, gm_ln_g[layer], gm_ws[layer], gm_bs[layer])
            ctx = ctx + cg1 * merge_branches(yc_a, yc_b, gac, gbc, w_proj_a[layer], w_proj_b[layer], w_out[layer])
            hc2 = modulate(rmsnorm_2(ctx, norm2_g[layer]), csh2, csc2)
            ctx = ctx + cg2 * peer_ffn(hc2, peer_wq[layer], peer_keys[layer], peer_u[layer], peer_v[layer])
    return rmsnorm_2(x, final_g)


def setup_inputs(seed=0):
    out = dict(first_inputs(seed))
    for name, value in second_inputs(seed + 1).items():
        if name != "x":
            out[name + "_2"] = value
    return out


def reference(
    x, attn_norm, ffn_norm, ev_w_in, ev_cmp_pos_k, ev_cmp_pos_v, ev_cmp_w_k, ev_cmp_w_v,
    ev_w_out, od_w_in, od_b_f, od_w_out, ffn_w_in, ffn_conv_w, ffn_conv_b, ffn_w_out,
    final_norm, c_2, ctx_2, c_ctx_2, ada_w_2, ada_b_2, norm1_g_2, norm2_g_2, w_in_2, na_rpb_2,
    gm_ln_g_2, gm_ws_2, gm_bs_2, w_proj_a_2, w_proj_b_2, w_out_2, peer_wq_2, peer_keys_2,
    peer_u_2, peer_v_2, final_g_2,
):
    x = first_block(
        x, attn_norm, ffn_norm, ev_w_in, ev_cmp_pos_k, ev_cmp_pos_v, ev_cmp_w_k, ev_cmp_w_v,
        ev_w_out, od_w_in, od_b_f, od_w_out, ffn_w_in, ffn_conv_w, ffn_conv_b, ffn_w_out,
        final_norm,
    )
    return second_block(
        x, c_2, ctx_2, c_ctx_2, ada_w_2, ada_b_2, norm1_g_2, norm2_g_2, w_in_2, na_rpb_2,
        gm_ln_g_2, gm_ws_2, gm_bs_2, w_proj_a_2, w_proj_b_2, w_out_2, peer_wq_2, peer_keys_2,
        peer_u_2, peer_v_2, final_g_2,
    )


_drawn_inputs = setup_inputs


def setup_inputs(seed=0):
    import zlib

    import numpy as np

    out = dict(_drawn_inputs(seed))
    spreads = {}
    factors = {'attn_norm': 2.957,
     'ev_cmp_pos_k': 8.0,
     'ffn_conv_b': 3.838,
     'final_norm': 2.691,
     'ctx_2': 6.579,
     'c_ctx_2': 4.355,
     'ada_b_2': 3.747,
     'norm1_g_2': 8.0,
     'norm2_g_2': 192.842,
     'na_rpb_2': 200.0,
     'gm_ln_g_2': 64.0,
     'gm_bs_2': 34.594,
     'w_proj_a_2': 2.861,
     'final_g_2': 178.181}
    for name, (base, spread) in spreads.items():
        noise = np.random.default_rng([zlib.crc32(name.encode()), seed]).standard_normal(out[name].shape)
        drawn = base * np.exp(spread * noise) if base else spread * noise
        out[name] = jnp.asarray(drawn.astype(out[name].dtype))
    for name, factor in factors.items():
        out[name] = (out[name] * factor).astype(out[name].dtype)
    return out
```

```python
from contextlib import ExitStack, contextmanager

import numpy as np

import concourse.bass as bass
from concourse import mybir

F32 = mybir.dt.float32
F32R = mybir.dt.float32r
BF16 = mybir.dt.bfloat16
U32 = mybir.dt.uint32
ALU = mybir.AluOpType
ACT = mybir.ActivationFunctionType
AX = mybir.AxisListType

P = 128
D = 1024
KT = D // P
T = 512
TT = T // P
DH = 64
FF = 2816
FFT = FF // P
FFH = FFT // 2
N_CMP = 31
CMP_LEN = 32
CTX = 256
CTT = CTX // P
N_ADA = 6 * KT
HK = 128
PEER_GROUPS = 16
TOK_BATCH = 32
N_BATCH = T // TOK_BATCH
SCALE = 0.125
NEG = -1e30
EPS = 1e-6

COLS = {}
_at = 0
for _name, _n in (("attn_norm", 16), ("ffn_norm", 16), ("final_norm", 8), ("norm1", 8), ("norm2", 8),
                  ("final_g", 8), ("conv_w", 2 * 3 * FFT), ("conv_b", 2 * FFT), ("b_f", 1), ("ada_b", N_ADA),
                  ("ln_g", 4), ("c", 16), ("pe_k", CMP_LEN), ("pe_v", CMP_LEN)):
    COLS[_name] = _at
    _at += _n
N_COLS = _at

TABS = {}
_at = 0
for _name, _n in (("cos", T), ("sin", T), ("cos_cmp", 32), ("sin_cmp", 32), ("perm", P), ("ident", P),
                  ("causal_neg", P), ("strict_t", P), ("tri", P), ("win_neg", DH), ("cmp_neg", TT * 32),
                  ("iota", P), ("iota16", 16)):
    TABS[_name] = _at
    _at += _n
N_TABS = _at


class Loop:
    def __init__(self, i, name, deltas):
        self.i, self.name, self.deltas = i, name, deltas


class Ticket:

    def __init__(self, sem, value, coef=0, loop=None):
        self.sem, self.value, self.coef, self.loop = sem, value, coef, loop


class Program:

    def __init__(self, nc, deltas):
        self.nc, self.deltas, self.found = nc, deltas, {}
        self.loop = None
        self.counters = []
        self.stack = ExitStack()
        self.waited = {}
        self.gates = {e.engine: self.stack.enter_context(nc.semaphore(n)) for n, e in (("dve_gate", nc.vector), ("pool_gate", nc.gpsimd))}
        self.pe, self.dve, self.act, self.pool = (Counter(self, n) for n in ("pe_done", "dve_done", "act_done", "pool_done"))

    def needs(self, engine, *tickets):
        for t in tickets:
            if t is None:
                continue
            if isinstance(t, (list, tuple)):
                self.needs(engine, *t)
                continue
            assert t.loop is None or t.loop is self.loop, "a ticket of a loop that has ended"
            if t.value <= 0 and t.coef == 0:
                continue
            key = (engine.engine, t.sem, t.loop.name if t.loop else None)
            assert t.value > 0, "a wait on a register's value has to be positive from the first pass on"
            if self.waited.get(key, 0) >= t.value:
                continue
            self.waited[key] = t.value
            engine.wait_ge(t.sem, t.value + t.loop.i * t.coef if t.loop and t.coef else t.value)

    def needs_first(self, engine, *tickets):
        self.needs(engine, *tickets)
        if self.loop:
            engine.sem_inc(self.gates[engine.engine], 1)

    @contextmanager
    def fori(self, name, n):
        start = [(c, c.n) for c in self.counters]
        deltas = self.deltas.get(name, {})
        self.waited = {}
        with self.nc.Fori(0, n) as i:
            self.loop = Loop(i, name, deltas)
            yield i
        self.found[name] = {c.name: c.n - s for c, s in start}
        self.loop = None
        self.waited = {}
        for c, s in start:
            c.n = s + n * (c.n - s)

    def delta(self, name):
        return self.loop.deltas.get(name, 0) if self.loop else 0


class Counter:

    def __init__(self, prog, name, step=1):
        self.prog, self.name, self.step, self.n = prog, name, step, 0
        self.sem = prog.stack.enter_context(prog.nc.semaphore(name))
        prog.counters.append(self)

    def did(self, ins):
        self.n += 1
        ins.then_inc(self.sem, self.step)
        return self.now()

    def now(self, back=0):
        p = self.prog
        return Ticket(self.sem, (self.n - back) * self.step, p.delta(self.name) * self.step, p.loop)


def run_together(*gens):
    live = [[g, k] for g, k in gens]
    while live:
        for entry in list(live):
            for _ in range(entry[1]):
                try:
                    next(entry[0])
                except StopIteration:
                    live.remove(entry)
                    break


def program(nc, io, deltas):
    pr = Program(nc, deltas)
    top = pr.stack
    needs, PE, DVE, AC, PO = pr.needs, pr.pe, pr.dve, pr.act, pr.pool
    te, ve, sc, gp, sy = nc.tensor, nc.vector, nc.scalar, nc.gpsimd, nc.sync

    def sb(stack, name, shape, dt=F32):
        return stack.enter_context(nc.sbuf_tensor(name, shape, dt))

    bank = [top.enter_context(nc.psum_tensor(f"bank{b}", [P, 512], F32)) for b in range(8)]
    lin = bank[0:2]
    s_bank, t_bank, o_bank, x_bank = bank[2:4], bank[4:6], bank[6], bank[7]
    WMAX = FFH * P
    w_raw = [sb(top, f"w_raw{s}", [P, WMAX]) for s in range(2)]
    w_hi = [sb(top, f"w_hi{s}", [P, WMAX], F32R) for s in range(2)]
    w_lo = [sb(top, f"w_lo{s}", [P, WMAX], F32R) for s in range(2)]
    x = sb(top, "x", [P, KT, T])
    h_hi = sb(top, "h_hi", [P, KT, T], F32R)
    h_lo = sb(top, "h_lo", [P, KT, T], F32R)
    cols = sb(top, "cols", [P, N_COLS])
    ident = sb(top, "ident", [P, P])
    ones = sb(top, "ones", [P, P])
    mod = sb(top, "mod", [P, N_ADA, 2])
    scaled_g = sb(top, "scaled_g", [P, 3, KT])

    w_in = [top.enter_context(nc.semaphore(f"weights_in{s}")) for s in range(2)]
    hi_done = Counter(pr, "weights_hi")
    lo_done = Counter(pr, "weights_lo")
    used = Counter(pr, "weights_used")
    plan = [("w8", 11 + 12 + 8)]
    for _ in range(2):
        plan += [("w8", 22), ("w11", 8), ("w8", 22), ("w11", 8)]
        if _ == 0:
            plan += [("w8", 1 + 24 + 8)]
    plan += [("w8", 12 + 8 + 24 + 8 + 16 + 256)]
    n_units = sum(n for _, n in plan)

    def load_weights():
        unit, at = 0, {"w8": 0, "w11": 0}

        def fetch(src, k, unit_base, row, after):
            slot = (unit_base + k) % 2
            if after is not None:
                sy.wait_ge(lo_done.sem, after)
            n = io[src].shape[2]
            sy.dma_start(w_raw[slot][:, 0:n], io[src][row, :, :].rearrange("a p n -> p (a n)") if not isinstance(row, int)
                         else io[src][row]).then_inc(w_in[slot], 16)

        for src, n in plan:
            done = 0
            while done < n and unit < 2:
                fetch(src, 0, unit, at[src], None)
                unit, done, at[src] = unit + 1, done + 1, at[src] + 1
            pairs = (n - done) // 2
            if pairs > 1:
                with sy.Fori(0, pairs) as j:
                    for k in range(2):
                        fetch(src, k, unit, bass.ds(j * 2 + (at[src] + k), 1), j * 2 + (unit + k - 1))
                unit, done, at[src] = unit + 2 * pairs, done + 2 * pairs, at[src] + 2 * pairs
            while done < n:
                fetch(src, 0, unit, at[src], unit - 1)
                unit, done, at[src] = unit + 1, done + 1, at[src] + 1

    def split_weights(blocks=KT):
        u = lo_done.n
        if pr.loop is None and u >= n_units:
            return
        slot, n = u % 2, blocks * P
        d = pr.delta("weights_lo")
        arrived = Ticket(w_in[slot], 16 * (u // 2 + 1), 8 * d, pr.loop)
        free = Ticket(used.sem, u - 1, d, pr.loop)
        needs(sc, arrived, free)
        hi = hi_done.did(sc.activation(w_hi[slot][:, 0:n], w_raw[slot][:, 0:n], ACT.Copy))
        needs(ve, arrived, free, hi)
        lo_done.did(ve.tensor_tensor(w_lo[slot][:, 0:n], w_raw[slot][:, 0:n], w_hi[slot][:, 0:n], ALU.subtract))

    lin_act = [Counter(pr, f"bank{b}_read_by_act") for b in range(2)]
    lin_dve = [Counter(pr, f"bank{b}_read_by_dve") for b in range(2)]

    def unit(b, groups, then=KT, before=()):
        u = used.n
        slot = u % 2
        split_weights(then)
        needs(te, Ticket(lo_done.sem, u + 1, pr.delta("weights_lo"), pr.loop), lin_act[b].now(), lin_dve[b].now(), *before)
        last = None
        for columns, blocks in groups:
            out = lin[b][:, columns] if isinstance(columns, slice) else columns
            for k, (w, hi, lo, *ready) in enumerate(blocks):
                needs(te, ready)
                wh, wl = w_hi[slot][:, w * P:(w + 1) * P], w_lo[slot][:, w * P:(w + 1) * P]
                te.matmul(out, wh, hi, start=(k == 0), stop=False)
                te.matmul(out, wh, lo, start=False, stop=False)
                last = te.matmul(out, wl, hi, start=False, stop=(k == len(blocks) - 1))
                if k % 2:
                    yield
        return used.did(last)

    def h_unit(b, **kw):
        return unit(b, [(slice(0, T), [(k, h_hi[:, k, :], h_lo[:, k, :], h_ready[k]) for k in range(KT)])], **kw)

    def now(gen):
        while True:
            try:
                next(gen)
            except StopIteration as e:
                return e.value

    def everything():
        return [c.now() for c in (PE, DVE, AC, PO, used, lo_done, hi_done, *lin_act, *lin_dve)]

    def all_but_pe():
        return [c.now() for c in (DVE, AC, PO, *lin_act, *lin_dve)]

    def barrier():
        t = everything()
        for e in (te, ve, sc, gp):
            needs(e, t)

    def split(hi, lo, src, *before):
        needs(sc, *before)
        a = AC.did(sc.activation(hi, src, ACT.Copy))
        needs(ve, *before)
        needs(ve, a)
        return DVE.did(ve.tensor_tensor(lo, src, hi, ALU.subtract))

    def col(name, k=0, n=1):
        return cols[:, COLS[name] + k:COLS[name] + k + n]

    def table_set(name):
        sc.preload_act_table_set(name)

    def dma_in(name, dst, src, engine=None):
        c = Counter(pr, name, 16)
        return c.did((engine or sc).dma_start(dst, src))

    load_weights()
    t_cols = dma_in("cols_in", cols[:, :], io["cols"])
    tabs = lambda name, n=None: io["tabs"][:, TABS[name]:TABS[name] + n]
    t_ident = dma_in("ident_in", ident[:, :], tabs("ident", P))
    t_x = dma_in("x_in", x[:, :, :], io["x"])
    t_ones = PO.did(gp.memset(ones[:, :], 1.0))

    acc = sb(top, "acc", [P, T])
    nv = sb(top, "norm_v", [P, T])
    ny = sb(top, "norm_y", [P, T])
    hf = [sb(top, f"norm_h{s}", [P, T]) for s in range(2)]
    h_ready = []

    def rstd_of(sums, n, denom, ready):
        v, y, t1 = nv[:, 0:n], ny[:, 0:n], acc[:, 0:n]
        needs(ve, ready)
        a = DVE.did(ve.tensor_scalar(v, sums, 1.0 / denom, EPS, ALU.mult, ALU.add))
        needs(ve, a)
        a = DVE.did(ve.reciprocal(t1, v))
        needs(sc, a)
        b = AC.did(sc.activation(y, t1, ACT.Sqrt))
        needs(ve, b)
        a = DVE.did(ve.tensor_tensor(t1, y, y, ALU.mult))
        needs(ve, a)
        a = DVE.did(ve.scalar_tensor_tensor(t1, v, -0.5, t1, ALU.mult, ALU.mult))
        needs(ve, a)
        return DVE.did(ve.scalar_tensor_tensor(y, t1, 1.5, y, ALU.add, ALU.mult))

    def clear_squares():
        pr.needs_first(gp, DVE.now(), PE.now(), AC.now())
        PO.did(gp.memset(acc[:, :], 0.0))

    def add_squares(k, src, t):
        needs(sc, t, PO.now(1))
        a = AC.did(sc.activation(hf[k % 2][:, :], src, ACT.Square))
        pr.needs_first(gp, a, PO.now())
        PO.did(gp.tensor_tensor(acc[:, :], acc[:, :], hf[k % 2][:, :], ALU.add))

    def total(out, n):
        needs(te, PO.now(), t_ones)
        return PE.did(te.matmul(out, ones[:, :], acc[:, 0:n], start=True, stop=True))

    def column_sums(src, tiles, n, out, square, ready):
        freed = [None, None]
        for k in range(tiles):
            if square:
                needs(sc, ready, freed[k % 2])
                a = AC.did(sc.activation(hf[k % 2][:, 0:n], src[:, k, :], ACT.Square))
                needs(te, a)
            else:
                needs(te, ready)
            moving = hf[k % 2][:, 0:n] if square else src[:, k, :]
            freed[k % 2] = PE.did(te.matmul(out, ones[:, :], moving, start=(k == 0), stop=(k == tiles - 1)))
        return freed[(tiles - 1) % 2]

    def norm(src, n, gain, shift, hi, lo, ready=None, have_squares=True):
        barrier()
        out = bank[2][:, 0:n]
        s = total(out, n) if have_squares else column_sums(src, KT, n, out, True, ready)
        r = rstd_of(out, n, D, s)
        done = []
        for k in range(KT):
            needs(ve, r, s, done[k - 2] if k >= 2 else None)
            t = DVE.did(ve.scalar_tensor_tensor(hf[k % 2][:, 0:n], src[:, k, :], gain(k), ny[:, 0:n], ALU.mult, ALU.mult))
            if shift is not None:
                needs(ve, t)
                t = DVE.did(ve.tensor_scalar(hf[k % 2][:, 0:n], hf[k % 2][:, 0:n], shift(k), None, ALU.add))
            done.append(split(hi[:, k, :], lo[:, k, :], hf[k % 2][:, 0:n], t))
        if hi is h_hi:
            h_ready[:] = done
        return done

    def norm_plain(gain, squares):
        barrier()
        r = rstd_of(bank[2][:, :], T, D, total(bank[2][:, :], T))
        if squares:
            clear_squares()
        for k in range(KT):
            needs(ve, r)
            a = DVE.did(ve.scalar_tensor_tensor(x[:, k, :], x[:, k, :], gain(k), ny[:, :], ALU.mult, ALU.mult))
            if squares:
                add_squares(k, x[:, k, :], a)

    ADA_STEP = 2
    ADA_STEPS = N_ADA // ADA_STEP // 2
    ADA_COLS = ADA_STEP * P

    def ada_units(st):
        silu = sb(st, "silu_c", [P, KT, 2])
        rows = sb(st, "ada_rows", [2, ADA_COLS])
        slot = [sb(st, f"ada_w{b}", [P, KT, ADA_COLS]) for b in range(2)]
        arrived = [Counter(pr, f"ada_in{b}", 16) for b in range(2)]
        needs(sc, t_cols)
        t_silu = AC.did(sc.activation(silu[:, :, :], col("c", 0, 16).rearrange("p (k c) -> p k c", c=2), ACT.Silu))

        def fetch(i, k, free):
            pr.needs_first(gp, free)
            arrived[k % 2].did(gp.dma_start(slot[k % 2][:, :, :], io["ada_w"][bass.ds(i * ADA_STEPS + k, 1), :, :, :]
                                            .rearrange("a p u n -> (a p) u n")))

        def steps(i, start, stop, entry):
            if start == 0:
                for k in range(2):
                    fetch(i, k, entry)
            read = entry
            for k in range(start, stop):
                needs(te, arrived[k % 2].now(), t_silu, read)
                for c in range(KT):
                    a = te.matmul(x_bank[0:2, 0:ADA_COLS], silu[:, c, :], slot[k % 2][:, c, :], start=(c == 0), stop=(c == KT - 1))
                    if c == KT - 1:
                        a = PE.did(a)
                    if c % 3 == 1:
                        yield
                if k + 2 < ADA_STEPS:
                    fetch(i, k + 2, a)
                needs(ve, a)
                b = DVE.did(ve.tensor_copy(rows[:, :], x_bank[0:2, 0:ADA_COLS]))
                yield
                needs(te, b, t_ident)
                for n in range(ADA_STEP):
                    a = te.matmul(x_bank[:, ADA_COLS + 2 * n:ADA_COLS + 2 * n + 2], rows[:, n * P:(n + 1) * P], ident[0:2, 0:2], start=True, stop=True)
                a = PE.did(a)
                yield
                needs(ve, a, t_cols)
                at = i * (N_ADA // 2) + k * ADA_STEP
                bias = cols[:, bass.ds(at + COLS["ada_b"], ADA_STEP)].unsqueeze(2).to_broadcast([P, ADA_STEP, 2])
                read = DVE.did(ve.tensor_tensor(mod[:, bass.ds(at, ADA_STEP), :],
                                                x_bank[:, ADA_COLS:ADA_COLS + 2 * ADA_STEP].rearrange("p (n c) -> p n c", c=2), bias, ALU.add))
        return steps

    def modulated_gains():
        needs(ve, everything())
        for row, (chunk, c, g) in enumerate(((1, 0, "norm1"), (1, 1, "norm1"), (4, 0, "norm2"))):
            DVE.did(ve.scalar_tensor_tensor(scaled_g[:, row, :], mod[:, chunk * KT:(chunk + 1) * KT, c], 1.0,
                                            col(g, 0, KT), ALU.add, ALU.mult))

    def out_units(i, hi, lo, gain=None, blocks=KT, thens=(KT, KT), squares=True, ready=None):
        for j in range(2):
            t = now(unit(j, [(slice(0, T), [(k, hi[:, k, :], lo[:, k, :], ready and ready[k]) for k in range(blocks)])], then=thens[j]))
            xs = x[:, bass.ds(i * 2 + j, 1), :]
            needs(ve, t)
            if gain is None:
                a = lin_dve[j].did(ve.tensor_tensor(xs, lin[j][:, :], xs, ALU.add))
            else:
                a = lin_dve[j].did(ve.scalar_tensor_tensor(xs, lin[j][:, :], gain(i * 2 + j), xs, ALU.mult, ALU.add))
            if squares:
                add_squares(j, xs, a)

    def out_proj(name, hi, lo, gain=None):
        clear_squares()
        with pr.fori(name, KT // 2) as i:
            out_units(i, hi, lo, gain)

    def to_natural(vT, v_nat, s, tiles, ready, freed, reader=None):
        needs(te, ready, freed, t_ident)
        for j in range(tiles):
            a = te.transpose(s[:, j * P:(j + 1) * P], vT[:, j * P:(j + 1) * P], ident[:, :])
        a = PE.did(a)
        needs(sc, a)
        return (reader or AC).did(sc.activation(v_nat, s[:, 0:tiles * P].rearrange("p (j d) -> p j d", j=tiles), ACT.Copy))

    def softmax_rows(S, Pm, width, small, k, scale, ready, guard=False, gate=None):
        mx, nm, rs, rc = (small[:, 4 * k + c:4 * k + c + 1] for c in range(4))
        needs(ve, ready)
        a = DVE.did(ve.tensor_reduce(mx, S, AX.X, ALU.max))
        needs(ve, a)
        a = DVE.did(ve.tensor_scalar(nm, mx, -1e20 if guard else -3e38, -scale, ALU.max, ALU.mult))
        needs(sc, a)
        read = a = AC.did(sc.activation(Pm, S, ACT.Exp, bias=nm, scale=scale, accum_out=rs))
        needs(ve, a)
        if guard:
            a = DVE.did(ve.tensor_scalar(rs, rs, 1e-30, None, ALU.max))
            needs(ve, a)
        a = DVE.did(ve.reciprocal(rc, rs))
        needs(ve, a)
        if gate is not None:
            a = DVE.did(ve.tensor_tensor(rc, rc, gate, ALU.mult))
            needs(ve, a)
        return DVE.did(ve.tensor_scalar(Pm, Pm, rc, None, ALU.mult)), read

    def even_phase():
        with ExitStack() as st:
            o_hi = sb(st, "o_hi", [P, KT, T], F32R)
            o_lo = sb(st, "o_lo", [P, KT, T], F32R)
            with ExitStack() as s2:
                nsa_phase(s2, o_hi, o_lo)
                barrier()
            with ExitStack() as s2:
                stick_phase(s2, o_hi, o_lo)
                barrier()
                modulated_gains()
            out_proj("ev_out", o_hi, o_lo)
            barrier()

    def nsa_phase(st, o_hi, o_lo):
        tab = sb(st, "rope_tab", [P, 2 * T + 64 + P])
        t_tab = dma_in("rope_in", tab[:, :], io["tabs"][:, TABS["cos"]:TABS["cos"] + 2 * T + 64 + P])
        cos, sin = tab[:, 0:T], tab[:, T:2 * T]
        cos_c, sin_c, perm = tab[:, 2 * T:2 * T + 32], tab[:, 2 * T + 32:2 * T + 64], tab[:, 2 * T + 64:]
        neg = sb(st, "nsa_neg", [P, P])
        t_neg = dma_in("nsa_neg_in", neg[:, :], tabs("causal_neg", P))
        cneg = sb(st, "cmp_neg", [P, TT, 32])
        t_cneg = dma_in("cmp_neg_in", cneg[:, :, :], tabs("cmp_neg", TT * 32).rearrange("p (t c) -> p t c", t=TT))
        gates = sb(st, "gates", [P, TT, 24])
        kc = sb(st, "kc", [P, 32])
        vc = sb(st, "vc", [32, P])
        keys = [sb(st, f"k_branch{b}", [P, T]) for b in range(2)]
        vals = [sb(st, f"v_branch{b}", [P, TT, P]) for b in range(2)]
        raw = sb(st, "nsa_raw", [P, T])
        ta = sb(st, "rope_a", [P, T])
        tb = sb(st, "rope_b", [P, T])

        def project(dst):
            b = used.n % 2
            t = now(h_unit(b))
            needs(sc, t)
            return lin_act[b].did(sc.activation(dst, lin[b][:, :], ACT.Copy))

        def rope(dst, src, n, c, s, scratch, r, freed):
            needs(te, r, t_tab, freed)
            a = PE.did(te.matmul(scratch, perm, src, start=True, stop=True))
            needs(ve, r, t_tab)
            b = DVE.did(ve.tensor_tensor(ta[:, 0:n], src, c, ALU.mult))
            needs(ve, a)
            d = DVE.did(ve.tensor_tensor(tb[:, 0:n], scratch, s, ALU.mult))
            needs(ve, b, d)
            return DVE.did(ve.tensor_tensor(dst, ta[:, 0:n], tb[:, 0:n], ALU.add))

        with ExitStack() as cs:
            cw = sb(cs, "cmp_w", [P, CMP_LEN, P])
            blk = sb(cs, "cmp_blocks", [P, CMP_LEN, 32])
            b = used.n % 2
            t = now(h_unit(b))
            needs(sc, t)
            a = lin_act[b].did(sc.activation(raw[0:24, :], lin[b][0:24, :], ACT.Sigmoid))
            needs(te, a, t_ident)
            for j in range(TT):
                a = te.transpose(x_bank[:, j * 32:j * 32 + 24], raw[0:24, j * P:(j + 1) * P], ident[0:24, 0:24])
            a = PE.did(a)
            needs(ve, a)
            t_gates = DVE.did(ve.tensor_copy(gates[:, :, :], x_bank[:, 0:P].rearrange("p (j c) -> p j c", j=TT)[:, :, 0:24]))
            prev = t_gates
            for which in range(2):
                w_ready = dma_in(f"cmp_w_in{which}", cw[:, :, :], io["cmp_w"][which]) if which == 0 else t_cw2
                needs(sc, prev, PE.now())
                a = project(raw[:, :])
                needs(ve, a, t_cols, prev)
                for half in range(2):
                    pe = cols[:, COLS["pe_k" if which == 0 else "pe_v"] + 16 * half:][:, 0:16]
                    b = DVE.did(ve.tensor_tensor(blk[:, 16 * half:16 * half + 16, 0:N_CMP],
                                                 raw[:, 16 * half:16 * half + 496].rearrange("p (c s) -> p s c", s=16),
                                                 pe.unsqueeze(2).to_broadcast([P, 16, N_CMP]), ALU.add))
                needs(te, b, w_ready)
                for l in range(CMP_LEN):
                    a = te.matmul(x_bank[:, 256:256 + N_CMP], cw[:, l, :], blk[:, l, 0:N_CMP], start=(l == 0), stop=(l == CMP_LEN - 1))
                a = PE.did(a)
                if which == 0:
                    needs(sc, a)
                    t_cw2 = dma_in("cmp_w_in1", cw[:, :, :], io["cmp_w"][1])
                needs(ve, a)
                b = DVE.did(ve.tensor_copy(tb[:, 256:256 + N_CMP], x_bank[:, 256:256 + N_CMP]))
                if which == 0:
                    prev = rope(kc[:, 0:N_CMP], tb[:, 256:256 + N_CMP], N_CMP, cos_c[:, 0:N_CMP], sin_c[:, 0:N_CMP],
                                x_bank[:, 384:384 + N_CMP], b, None)
                    t_kc = prev
                else:
                    needs(te, b)
                    a = PE.did(te.transpose(x_bank[0:N_CMP, 0:P], tb[:, 256:256 + N_CMP], ident[:, :]))
                    needs(ve, a)
                    t_vc = DVE.did(ve.tensor_copy(vc[0:N_CMP, :], x_bank[0:N_CMP, 0:P]))
            free = t_vc
            for b in range(2):
                needs(sc, free)
                free = rope(keys[b][:, :], raw[:, :], T, cos, sin, t_bank[0][:, :], project(raw[:, :]), None)
            for b in range(2):
                needs(sc, free)
                free = to_natural(raw, vals[b][:, :, :], t_bank[b][:, :], TT, project(raw[:, :]), None)
                needs(sc, PE.now())
            barrier()

        q = [sb(st, f"nsa_q{s}", [P, T]) for s in range(2)]
        Pm = [[sb(st, f"nsa_p{hh}{b}", [P, T]) for b in range(3)] for hh in range(2)]
        PT = [[sb(st, f"nsa_pt{hh}{b}", [P, TT, P]) for b in range(3)] for hh in range(2)]
        small = [sb(st, f"nsa_small{hh}", [P, 12]) for hh in range(2)]

        q_ready = [None, None]

        def project_q(s, entry):
            b = used.n % 2
            t = yield from h_unit(b)
            needs(sc, t, *entry)
            a = lin_act[b].did(sc.activation(raw[:, :], lin[b][:, :], ACT.Copy))
            yield
            q_ready[s] = rope(q[s][:, :], raw[:, :], T, cos, sin, x_bank[:, :], a, entry)

        def head(hh, s, gate, entry):
            rows = slice(hh * DH, hh * DH + DH)
            S, Tb, sm = s_bank[hh], t_bank[hh], small[hh]
            last_pv = entry
            for i in range(TT):
                kw = (i + 1) * P
                ready = []
                s_read = last_pv
                for b, (key, w) in enumerate(((kc, N_CMP), (keys[0], kw), (keys[1], kw))):
                    needs(te, q_ready[s], s_read, t_kc)
                    a = PE.did(te.matmul(S[:, 0:w], q[s][rows, i * P:(i + 1) * P], key[rows, 0:w], start=True, stop=True))
                    yield
                    needs(ve, a, t_cneg, t_neg, last_pv)
                    part = S[:, 0:w] if b == 0 else S[:, i * P:(i + 1) * P]
                    a = DVE.did(ve.tensor_tensor(part, part, cneg[:, i, 0:w] if b == 0 else neg[:, :], ALU.add))
                    needs(sc, last_pv)
                    yield
                    p_ready, s_read = softmax_rows(S[:, 0:w], Pm[hh][b][:, 0:w], w, sm, b, SCALE, a, b == 0, gates[:, i, gate(hh, b)])
                    ready.append(p_ready)
                    yield
                t_read = last_pv
                for b, w in enumerate((N_CMP, kw, kw)):
                    needs(te, ready[b], t_read)
                    for j in range(0, w, P):
                        n = min(P, w - j)
                        a = te.transpose(Tb[0:n, j:j + P], Pm[hh][b][:, j:j + n], ident[:, :])
                    a = PE.did(a)
                    needs(sc, a, last_pv)
                    n = min(P, w)
                    t_read = AC.did(sc.activation(PT[hh][b][0:n, 0:(w + P - 1) // P, :],
                                                  Tb[0:n, 0:max(w, P)].rearrange("p (j q) -> p j q", q=P), ACT.Copy))
                    yield
                needs(te, t_read, t_vc, *entry)
                out = o_bank[rows, i * P:(i + 1) * P]
                te.matmul(out, vc[0:N_CMP, rows], PT[hh][0][0:N_CMP, 0, :], start=True, stop=False)
                for b in range(2):
                    for j in range(i + 1):
                        a = te.matmul(out, vals[b][:, j, rows], PT[hh][b + 1][:, j, :], start=False, stop=(b == 1 and j == i))
                last_pv = [PE.did(a)]
                yield

        def pair_out(pair):
            return split(o_hi[:, pair, :], o_lo[:, pair, :], o_bank[:, :], PE.now())

        table_set("exp_and_others")
        with pr.fori("nsa", 2) as i:
            entry = everything()
            q_ready[:] = [None, None]
            now(project_q(0, entry))

            def gate(s):
                return lambda hh, b: bass.ds((i * 2 + s) * 3 + (12 * hh + b), 1)

            run_together((head(0, 0, gate(0), entry), 1), (head(1, 0, gate(0), entry), 1), (project_q(1, entry), 1))
            t = pair_out(bass.ds(i * 2 + 4, 1))
            run_together((head(0, 1, gate(1), [t]), 1), (head(1, 1, gate(1), [t]), 1))
            pair_out(bass.ds(i * 2 + 5, 1))

    def project_pair(bufs, s, entry):
        q, k, v, vT = bufs
        for dst in (q[s], k[s], vT):
            b = used.n % 2
            t = yield from h_unit(b)
            needs(sc, t, *entry)
            a = lin_act[b].did(sc.activation(dst[:, :], lin[b][:, :], ACT.Copy))
            yield
        return to_natural(vT, v[s][:, :, :], lin[b], TT, a, a, lin_act[b])

    def stick_phase(st, o_hi, o_lo):
        q = [sb(st, f"sb_q{s}", [P, T]) for s in range(2)]
        k = [sb(st, f"sb_k{s}", [P, T]) for s in range(2)]
        v = [sb(st, f"sb_v{s}", [P, TT, P]) for s in range(2)]
        vT = sb(st, "sb_vT", [P, T])
        strict = sb(st, "strict", [P, P])
        tri = sb(st, "tri", [P, P])
        t_strict = dma_in("strict_in", strict[:, :], tabs("strict_t", P))
        t_tri = dma_in("tri_in", tri[:, :], tabs("tri", P))
        work = [[sb(st, f"sb_{nm}{hh}", [P, T]) for nm in ("t", "ls", "lk", "a")] for hh in range(2)]
        later = [sb(st, f"sb_later{hh}", [P, T]) for hh in range(2)]
        ready = [None, None]
        ada = ada_units(st)

        def project(s, entry):
            ready[s] = yield from project_pair((q, k, v, vT), s, entry)

        def head(hh, s, entry):
            rows = slice(hh * DH, hh * DH + DH)
            tt, ls, lk, aw = work[hh]
            Z, A = s_bank[hh], t_bank[hh]
            prev = entry
            for n, j in enumerate(reversed(range(TT))):
                lo = j * P
                w = slice(lo, T)
                needs(te, ready[s], *prev)
                a = PE.did(te.matmul(Z[:, w], k[s][rows, lo:lo + P], q[s][rows, w], start=True, stop=True))
                yield
                needs(sc, a, *prev)
                z_abs = b = AC.did(sc.activation(tt[:, w], Z[:, w], ACT.Abs, scale=SCALE))
                needs(sc, b)
                b = AC.did(sc.activation(tt[:, w], tt[:, w], ACT.Exp, scale=-1.0))
                yield
                needs(sc, b)
                b = AC.did(sc.activation(tt[:, w], tt[:, w], ACT.Ln, bias=1.0))
                needs(ve, z_abs, *prev)
                c = DVE.did(ve.tensor_scalar(ls[:, w], Z[:, w], SCALE, 0.0, ALU.mult, ALU.min))
                yield
                needs(ve, b, c)
                c = DVE.did(ve.tensor_tensor(ls[:, w], ls[:, w], tt[:, w], ALU.subtract))
                needs(ve, c)
                c = DVE.did(ve.scalar_tensor_tensor(lk[:, w], Z[:, w], -SCALE, ls[:, w], ALU.mult, ALU.add))
                yield
                needs(gp, c, t_strict)
                m = PO.did(gp.tensor_tensor(lk[:, lo:lo + P], lk[:, lo:lo + P], strict[:, :], ALU.mult))
                needs(te, m, t_tri)
                a = te.matmul(A[:, w], tri[:, :], lk[:, w], start=True, stop=(n == 0))
                if n:
                    a = te.matmul(A[:, lo + P:T], ones[:, :], later[hh][:, lo + P:T], start=False, stop=True)
                a = PE.did(a)
                pr.needs_first(gp, m, a)
                if n:
                    PO.did(gp.tensor_copy(later[hh][:, lo:lo + P], lk[:, lo:lo + P]))
                    m2 = PO.did(gp.tensor_tensor(later[hh][:, lo + P:T], later[hh][:, lo + P:T], lk[:, lo + P:T], ALU.add))
                else:
                    m2 = PO.did(gp.tensor_copy(later[hh][:, w], lk[:, w]))
                yield
                needs(ve, a)
                c = DVE.did(ve.tensor_tensor(ls[:, w], A[:, w], ls[:, w], ALU.add))
                needs(sc, c)
                b = AC.did(sc.activation(aw[:, w], ls[:, w], ACT.Exp))
                yield
                needs(gp, b)
                m3 = PO.did(gp.tensor_tensor(aw[:, lo:lo + P], aw[:, lo:lo + P], strict[:, :], ALU.mult))
                needs(te, b, m3)
                a = te.matmul(o_bank[rows, lo:lo + P], v[s][:, j, rows], aw[:, lo:lo + P], start=(n == 0), stop=False)
                if n:
                    a = te.matmul(o_bank[rows, lo + P:T], v[s][:, j, rows], aw[:, lo + P:T], start=False, stop=(j == 0))
                a = PE.did(a)
                prev = [a, m2, m3]
                yield

        def pair_out(pair):
            return split(o_hi[:, pair, :], o_lo[:, pair, :], o_bank[:, :], PE.now())

        table_set("natural_log_exp_and_others")
        with pr.fori("stick", 2) as i:
            entry = everything()
            now(project(0, entry))
            run_together((head(0, 0, entry), 1), (head(1, 0, entry), 1), (project(1, entry), 1), (ada(i, 0, ADA_STEPS // 2, entry), 1))
            t = pair_out(bass.ds(i * 2, 1))
            run_together((head(0, 1, [t]), 1), (head(1, 1, [t]), 1), (ada(i, ADA_STEPS // 2, ADA_STEPS, [DVE.now()]), 1))
            pair_out(bass.ds(i * 2 + 1, 1))

    def ffn_phase(layer):
        with ExitStack() as st:
            g_hi = sb(st, f"g_hi{layer}", [P, FFH, T], F32R)
            g_lo = sb(st, f"g_lo{layer}", [P, FFH, T], F32R)
            a_in = sb(st, f"a_in{layer}", [P, T + 2])
            cv = [sb(st, f"cv{layer}{s}", [P, T]) for s in range(2)]
            gf = sb(st, f"gf{layer}", [P, T])
            needs(ve, t_cols)
            DVE.did(ve.memset(a_in[:, 0:2], 0.0))

            def hidden_tile(f, dst, then=KT):
                base = COLS["conv_w"] + layer * 3 * FFT
                tap = lambda n: cols[:, bass.ds(f + (base + n * FFT), 1)]
                bias = cols[:, bass.ds(f + (COLS["conv_b"] + layer * FFT), 1)]
                before = [DVE.now(), AC.now()]
                t = now(h_unit(0))
                needs(sc, t, *before)
                a = lin_act[0].did(sc.activation(a_in[:, 2:T + 2], lin[0][:, :], ACT.Copy))
                t2 = now(h_unit(1, then=then))
                needs(ve, a, *before)
                c = DVE.did(ve.tensor_scalar(cv[0][:, :], a_in[:, 0:T], tap(0), None, ALU.mult))
                needs(ve, c)
                c = DVE.did(ve.scalar_tensor_tensor(cv[1][:, :], a_in[:, 1:T + 1], tap(1), cv[0][:, :], ALU.mult, ALU.add))
                needs(ve, c)
                c = DVE.did(ve.scalar_tensor_tensor(cv[0][:, :], a_in[:, 2:T + 2], tap(2), cv[1][:, :], ALU.mult, ALU.add))
                needs(sc, c)
                a = AC.did(sc.activation(cv[1][:, :], cv[0][:, :], ACT.Silu, bias=bias))
                needs(ve, a, t2)
                c = lin_dve[1].did(ve.tensor_tensor(gf[:, :], lin[1][:, :], cv[1][:, :], ALU.mult))
                return split(g_hi[:, dst, :], g_lo[:, dst, :], gf[:, :], c)

            for half in range(2):
                table_set("silu_and_others")
                with pr.fori(f"ffn_in{layer}{half}", FFH - 1) as i:
                    hidden_tile(i + half * FFH, bass.ds(i, 1))
                tiles_in = DVE.now()
                last = hidden_tile(half * FFH + FFH - 1, FFH - 1, then=FFH)
                out_ready = [tiles_in] * (FFH - 1) + [last]
                if half:
                    clear_squares()
                with pr.fori(f"ffn_out{layer}{half}", KT // 2 - 1) as i:
                    out_units(i, g_hi, g_lo, blocks=FFH, thens=(FFH, FFH), squares=half == 1, ready=out_ready)
                out_units(KT // 2 - 1, g_hi, g_lo, blocks=FFH, thens=(FFH, KT), squares=half == 1, ready=out_ready)
                if half:
                    barrier()

    def odd_phase():
        with ExitStack() as st:
            o_hi = sb(st, "fo_hi", [P, KT, T], F32R)
            o_lo = sb(st, "fo_lo", [P, KT, T], F32R)
            with ExitStack() as s2:
                fox_phase(s2, o_hi, o_lo)
                barrier()
            out_proj("od_out", o_hi, o_lo)
            barrier()

    def fox_phase(st, o_hi, o_lo):
        q = [sb(st, f"fx_q{s}", [P, T]) for s in range(2)]
        k = [sb(st, f"fx_k{s}", [P, T]) for s in range(2)]
        v = [sb(st, f"fx_v{s}", [P, TT, P]) for s in range(2)]
        vT = sb(st, "fx_vT", [P, T])
        neg = sb(st, "fx_neg", [P, P])
        t_neg = dma_in("fx_neg_in", neg[:, :], tabs("causal_neg", P))
        cum = sb(st, "fx_cum", [P, T])
        u = sb(st, "fx_u", [P, T])
        z = sb(st, "fx_z", [P, T])
        Pm = [[sb(st, f"fx_p{hh}{b}", [P, T]) for b in range(2)] for hh in range(2)]
        PT = [[sb(st, f"fx_pt{hh}{b}", [P, TT, P]) for b in range(2)] for hh in range(2)]
        small = [sb(st, f"fx_small{hh}", [P, 8]) for hh in range(2)]
        row = sb(st, "fx_row", [P, T])
        fb = used.n % 2
        t = now(h_unit(fb))
        needs(sc, t, t_cols)
        needs(ve, t, t_cols)
        b_f = col("b_f")
        a = lin_act[fb].did(sc.activation(u[:, :], lin[fb][:, :], ACT.Abs, bias=b_f))
        needs(ve, a)
        needs(sc, a)
        a = AC.did(sc.activation(u[:, :], u[:, :], ACT.Exp, scale=-1.0))
        needs(sc, a)
        a = AC.did(sc.activation(u[:, :], u[:, :], ACT.Ln, bias=1.0))
        c = lin_dve[fb].did(ve.tensor_scalar(z[:, :], lin[fb][:, :], b_f, 0.0, ALU.add, ALU.min))
        needs(ve, a, c)
        c = DVE.did(ve.tensor_tensor(z[:, :], z[:, :], u[:, :], ALU.subtract))
        needs(ve, c)
        c = DVE.did(ve.memset(u[:, :], 1.0))
        needs(ve, c)
        c = DVE.did(ve.tensor_tensor_scan(cum[:, :], u[:, :], z[:, :], 0.0, ALU.mult, ALU.add))
        needs(ve, c)
        t_cum = DVE.did(ve.tensor_scalar(cum[:, :], cum[:, :], -1.0 / SCALE, None, ALU.mult))
        ready = [None, None]

        def project(s, entry):
            ready[s] = yield from project_pair((q, k, v, vT), s, entry)

        def head(hh, s, pick, entry):
            rows = slice(hh * DH, hh * DH + DH)
            needs(ve, t_cum, t_ident, *entry)
            c = DVE.did(ve.tensor_scalar(row[rows, :], cum[rows, :], pick(hh), None, ALU.mult))
            Tb, sm = t_bank[hh], small[hh]
            S = s_bank[hh]
            s_free, pt_free, t_free = list(entry), [None, None], list(entry)
            for i in range(TT):
                kw = (i + 1) * P
                Pb, PTb = Pm[hh][i % 2], PT[hh][i % 2]
                needs(te, ready[s], c, *s_free)
                te.matmul(S[:, 0:kw], q[s][rows, i * P:(i + 1) * P], k[s][rows, 0:kw], start=True, stop=False)
                a = PE.did(te.matmul(S[:, 0:kw], ones[rows, :], row[rows, 0:kw], start=False, stop=True))
                yield
                needs(ve, a, t_neg)
                diag = S[:, i * P:(i + 1) * P]
                a = DVE.did(ve.tensor_tensor(diag, diag, neg[:, :], ALU.add))
                needs(sc, pt_free[i % 2], *entry)
                yield
                pd, s_read = softmax_rows(S[:, 0:kw], Pb[:, 0:kw], kw, sm, i % 2, SCALE, a)
                s_free = [s_read]
                yield
                needs(te, pd, *t_free)
                for j in range(i + 1):
                    a = te.transpose(Tb[:, j * P:(j + 1) * P], Pb[:, j * P:(j + 1) * P], ident[:, :])
                a = PE.did(a)
                needs(sc, a, pt_free[i % 2], *entry)
                b = AC.did(sc.activation(PTb[:, 0:i + 1, :], Tb[:, 0:kw].rearrange("p (j q) -> p j q", q=P), ACT.Copy))
                t_free = [b]
                yield
                needs(te, b, *entry)
                for j in range(i + 1):
                    a = te.matmul(o_bank[rows, i * P:(i + 1) * P], v[s][:, j, rows], PTb[:, j, :], start=(j == 0), stop=(j == i))
                pt_free[i % 2] = PE.did(a)
                yield

        def pair_out(pair):
            return split(o_hi[:, pair, :], o_lo[:, pair, :], o_bank[:, :], PE.now())

        def pick(pair):
            return lambda hh: ident[hh * DH:hh * DH + DH, bass.ds(pair * 2 + (hh + hh * DH), 1)]

        now(project(0, everything()))

        def two_pairs(i, more):
            entry = everything()
            ready[:] = [None, None]
            needs(te, entry)
            run_together((head(0, 0, pick(i * 2), entry), 1), (head(1, 0, pick(i * 2), entry), 1), (project(1, entry), 1))
            t = pair_out(bass.ds(i * 2, 1))
            gens = [(head(0, 1, pick(i * 2 + 1), [t]), 1), (head(1, 1, pick(i * 2 + 1), [t]), 1)]
            if more:
                gens.append((project(0, [t]), 1))
            run_together(*gens)
            pair_out(bass.ds(i * 2 + 1, 1))

        table_set("exp_and_others")
        with pr.fori("fox", 3) as i:
            two_pairs(i, True)
        two_pairs(3, False)

    NK = T + CTX
    NKT = NK // P

    def neighbour_phase(st, y_hi, y_lo):
        hc_hi = sb(st, "hc_hi", [P, KT, CTX], F32R)
        hc_lo = sb(st, "hc_lo", [P, KT, CTX], F32R)
        with ExitStack() as s2:
            cx = sb(s2, "ctx_x", [P, KT, CTX])
            t_cx = dma_in("ctx_in", cx[:, :, :], io["ctx"])
            norm(cx, CTX, lambda k: scaled_g[:, 1, k:k + 1], lambda k: mod[:, k, 1:2], hc_hi, hc_lo, t_cx, False)
            barrier()
        q = [sb(st, f"na_q{s}", [P, T]) for s in range(2)]
        k = [sb(st, f"na_k{s}", [P, NK]) for s in range(2)]
        v = [sb(st, f"na_v{s}", [P, NKT, P]) for s in range(2)]
        vT = sb(st, "na_vT", [P, NK])
        bias = [sb(st, f"na_bias{s}", [P, 2 * 14, DH]) for s in range(2)]
        win = sb(st, "na_win", [P, DH])
        t_win = dma_in("win_in", win[:, :], tabs("win_neg", DH))
        sc_sb = [sb(st, f"na_s{hh}", [P, NK]) for hh in range(2)]
        Pm = [sb(st, f"na_p{hh}", [P, NK]) for hh in range(2)]
        PT = [sb(st, f"na_pt{hh}", [P, NKT, P]) for hh in range(2)]
        small = [sb(st, f"na_small{hh}", [P, 4]) for hh in range(2)]
        bias_in = [Counter(pr, f"na_bias_in{s}", 16) for s in range(2)]
        main = (slice(0, T), [(kk, h_hi[:, kk, :], h_lo[:, kk, :], h_ready[kk]) for kk in range(KT)])
        ready, b_ready = [None, None], [None, None]

        xb_read = [None]

        def project(s, pair, entry):
            needs(sc, *entry)
            t = bias_in[s].did(sc.dma_start(bias[s][:, :, :], io["bias"][pair].rearrange("a p (d c) -> p (a d) c", c=DH)))
            for n, dst in enumerate((q[s], k[s], vT)):
                b = used.n % 2
                xb = x_bank[:, (n - 1) * CTX:n * CTX] if n else None
                more = [(xb, [(kk, hc_hi[:, kk, :], hc_lo[:, kk, :]) for kk in range(KT)])] if n else []
                a = yield from unit(b, [main] + more, before=[*entry, xb_read[0]])
                needs(sc, a)
                a = lin_act[b].did(sc.activation(dst[:, 0:T], lin[b][:, :], ACT.Copy))
                if n:
                    xb_read[0] = a = AC.did(sc.activation(dst[:, T:NK], xb, ACT.Copy))
                yield
            a1 = to_natural(vT, v[s][:, 0:TT, :], lin[b], TT, [a, lin_act[b].now()], None, lin_act[b])
            xb_read[0] = a2 = to_natural(vT[:, T:NK], v[s][:, TT:NKT, :], x_bank, CTT, a, None)
            yield
            needs(ve, t, t_win)
            b_ready[s] = DVE.did(ve.tensor_tensor(bias[s][:, :, :], bias[s][:, :, :],
                                                  win[:, :].unsqueeze(1).to_broadcast([P, 28, DH]), ALU.add))
            ready[s] = [a1, a2]

        def head(hh, s, entry):
            rows = slice(hh * DH, hh * DH + DH)
            S, Tb = s_bank[hh], t_bank[hh]
            last = list(entry)
            for i in range(TT):
                needs(te, ready[s], *last)
                lhs = q[s][rows, i * P:(i + 1) * P]
                te.matmul(S[:, :], lhs, k[s][rows, 0:T], start=True, stop=True)
                a = PE.did(te.matmul(Tb[:, 0:CTX], lhs, k[s][rows, T:NK], start=True, stop=True))
                yield
                needs(ve, a, b_ready[s], *last)
                e0 = 14 * hh + 6 - 2 * i
                c = DVE.did(ve.scalar_tensor_tensor(sc_sb[hh][:, 0:T], S[:, :], SCALE,
                                                    bias[s][:, e0:e0 + 8, :].rearrange("p d c -> p (d c)"), ALU.mult, ALU.add))
                needs(sc, a, *last)
                b = AC.did(sc.activation(sc_sb[hh][:, T:NK], Tb[:, 0:CTX], ACT.Copy, scale=SCALE))
                yield
                pd, _ = softmax_rows(sc_sb[hh][:, :], Pm[hh][:, :], NK, small[hh], 0, 1.0, [b, c])
                yield
                needs(te, pd, c, b)
                for j in range(TT):
                    te.transpose(Tb[:, j * P:(j + 1) * P], Pm[hh][:, j * P:(j + 1) * P], ident[:, :])
                for j in range(CTT):
                    a = te.transpose(S[:, j * P:(j + 1) * P], Pm[hh][:, T + j * P:T + (j + 1) * P], ident[:, :])
                a = PE.did(a)
                needs(sc, a, *last)
                AC.did(sc.activation(PT[hh][:, 0:TT, :], Tb[:, :].rearrange("p (j q) -> p j q", q=P), ACT.Copy))
                b = AC.did(sc.activation(PT[hh][:, TT:NKT, :], S[:, 0:CTX].rearrange("p (j q) -> p j q", q=P), ACT.Copy))
                yield
                needs(te, b)
                for j in range(NKT):
                    a = te.matmul(o_bank[rows, i * P:(i + 1) * P], v[s][:, j, rows], PT[hh][:, j, :], start=(j == 0), stop=(j == NKT - 1))
                last = [PE.did(a)]
                yield

        def pair_out(pair):
            return split(y_hi[:, pair, :], y_lo[:, pair, :], o_bank[:, :], PE.now())

        table_set("exp_and_others")
        with pr.fori("neighbour", 2) as i:
            entry = everything()
            ready[:], b_ready[:], xb_read[:] = [None, None], [None, None], [None]
            now(project(0, bass.ds(i * 2, 1), entry))
            run_together((head(0, 0, entry), 1), (head(1, 0, entry), 1), (project(1, bass.ds(i * 2 + 1, 1), [*entry, *everything()]), 1))
            t = pair_out(bass.ds(i * 2, 1))
            run_together((head(0, 1, [t]), 1), (head(1, 1, [t]), 1))
            pair_out(bass.ds(i * 2 + 1, 1))
        barrier()

    CT = 4

    def gating_phase(st, y_hi, y_lo):
        gv = sb(st, "gv", [P, CT, T])
        u = sb(st, "gu", [P, CT, T])
        vn = sb(st, "vn", [P, TT, CT * P])
        wsT = sb(st, "wsT", [P, 8, P])
        bs = sb(st, "bs", [P, CT, P])
        t_ws = dma_in("ws_in", wsT[:, :, :], io["ws"])
        t_bs = dma_in("bs_in", bs[:, :, :], io["bs"])
        table_set("gelu_apprx_tanh_and_others")
        for name, dst in (("gv", gv), ("gu", u)):
            with pr.fori(name, CT // 2) as i:
                for j in range(2):
                    t = now(h_unit(j))
                    needs(sc, t)
                    lin_act[j].did(sc.activation(dst[:, bass.ds(i * 2 + j, 1), :], lin[j][:, :], ACT.Gelu_apprx_tanh))
        barrier()
        with ExitStack() as s2:
            mean = sb(s2, "ln_mean", [P, T])
            s = column_sums(gv, CT, T, bank[2][:, :], False, None)
            needs(ve, s)
            a = DVE.did(ve.tensor_scalar(mean[:, :], bank[2][:, :], 1.0 / (CT * P), None, ALU.mult))
            needs(ve, a)
            for k in range(CT):
                a = DVE.did(ve.tensor_tensor(gv[:, k, :], gv[:, k, :], mean[:, :], ALU.subtract))
            s = column_sums(gv, CT, T, bank[3][:, :], True, a)
            r = rstd_of(bank[3][:, :], T, CT * P, s)
            needs(ve, r)
            for k in range(CT):
                a = DVE.did(ve.scalar_tensor_tensor(gv[:, k, :], gv[:, k, :], col("ln_g", k), ny[:, :], ALU.mult, ALU.mult))
            for n in range(TT):
                b = t_bank[n % 2]
                needs(te, a, AC.now(1) if n >= 2 else None)
                for k in range(CT):
                    c = te.transpose(b[:, k * P:(k + 1) * P], gv[:, k, n * P:(n + 1) * P], ident[:, :])
                c = PE.did(c)
                needs(sc, c)
                t_vn = AC.did(sc.activation(vn[:, n, :], b[:, :], ACT.Copy))
            tmp = [sb(s2, f"mix{k}", [P, T]) for k in range(2)]
            done = [None, None]
            for k in range(CT):
                b = s_bank[k % 2]
                needs(te, t_vn, t_ws, r, done[k % 2])
                for g2 in range(2):
                    for n in range(TT):
                        c = te.matmul(b[g2 * DH:(g2 + 1) * DH, n * P:(n + 1) * P], vn[:, n, k * P + g2 * DH:k * P + (g2 + 1) * DH],
                                      wsT[:, 2 * k + g2, :], start=True, stop=True)
                c = PE.did(c)
                needs(ve, c, t_bs, done[k % 2])
                c = DVE.did(ve.tensor_tensor(tmp[k % 2][:, :].rearrange("p (n q) -> p n q", n=TT), b[:, :].rearrange("p (n q) -> p n q", n=TT),
                                             bs[:, k, :].unsqueeze(1).to_broadcast([P, TT, P]), ALU.add))
                needs(ve, c)
                c = DVE.did(ve.tensor_tensor(tmp[k % 2][:, :], tmp[k % 2][:, :], u[:, k, :], ALU.mult))
                done[k % 2] = split(y_hi[:, k, :], y_lo[:, k, :], tmp[k % 2][:, :], c)
            barrier()

    def merge_phase(st, a_hi, a_lo, b_hi, b_lo, m_hi, m_lo):
        ga = sb(st, "ga", [P, T])
        gb = sb(st, "gb", [P, T])
        m = sb(st, "m", [P, T])
        table_set("sigmoid_and_others")
        with pr.fori("merge", KT // 2) as i:
            free = [DVE.now(), AC.now()]
            for j in range(2):
                for dst in (ga, gb):
                    b = used.n % 2
                    t = now(h_unit(b))
                    needs(sc, t, *free)
                    s = lin_act[b].did(sc.activation(dst[:, :], lin[b][:, :], ACT.Sigmoid))
                b = used.n % 2
                t = now(unit(b, [(slice(0, T), [(k, a_hi[:, k, :], a_lo[:, k, :]) for k in range(CT)]),
                                 (x_bank[:, :], [(CT + k, b_hi[:, k, :], b_lo[:, k, :]) for k in range(CT)])], before=free))
                needs(ve, t, s, lin_act[0].now(), lin_act[1].now())
                c = lin_dve[b].did(ve.tensor_tensor(ga[:, :], lin[b][:, :], ga[:, :], ALU.mult))
                d = DVE.did(ve.tensor_tensor(gb[:, :], x_bank[:, :], gb[:, :], ALU.mult))
                needs(ve, c, d, *free)
                d = DVE.did(ve.tensor_tensor(m[:, :], ga[:, :], gb[:, :], ALU.add))
                dst = bass.ds(i * 2 + j, 1)
                free = [split(m_hi[:, dst, :], m_lo[:, dst, :], m[:, :], d)]
        barrier()

    mod_flat = mod[:, :, :].rearrange("p a c -> p (a c)")
    H8 = 8
    K16 = 16
    G_TOK = 16
    G_BATCH = T // G_TOK
    g_dram = nc.dram_tensor("expert_weights", (G_BATCH, P, HK, G_TOK), F32).ap()

    def top16(vals, index, src, work, ready):
        first = pr.needs_first
        first(ve, ready)
        a = DVE.did(ve.max(vals[0], src))
        first(ve, a)
        DVE.did(ve.max_index(index[0], vals[0], src))
        a = DVE.did(ve.match_replace(work, vals[0], src, -3e38))
        first(ve, a)
        a = DVE.did(ve.max(vals[1], work))
        first(ve, a)
        return DVE.did(ve.max_index(index[1], vals[1], work))

    def peer_phase():
        with ExitStack() as st:
            gT = sb(st, "gT", [P, T])
            iT = sb(st, "iT", [P, T])
            jT = sb(st, "jT", [P, T])
            with ExitStack() as s2:
                retrieve(s2, gT, iT, jT)
                barrier()
            with ExitStack() as s2:
                scatter(s2, gT, iT, jT)
                barrier()
        with ExitStack() as st:
            experts(st)
            barrier()

    def retrieve(st, gT, iT, jT):
        keysT = sb(st, "keysT", [P, 16, P])
        t_keys = dma_in("keys_in", keysT[:, :, :], io["keys"])
        iota16 = sb(st, "iota16", [P, K16])
        t_iota = dma_in("iota16_in", iota16[:, :], tabs("iota16", K16))
        qT = [sb(st, f"pq{j}", [P, T]) for j in range(2)]
        s_sb = [sb(st, f"ps{j}", [P, TT, P]) for j in range(2)]
        work = sb(st, "pwork", [P, 256])
        vals = sb(st, "pvals", [P, TT, 16, K16])
        index = sb(st, "pindex", [P, TT, 16, K16], U32)
        two_v = sb(st, "ptwo_v", [P, TT, 2, K16])
        two_i = sb(st, "ptwo_i", [P, TT, 2, K16], U32)
        with pr.fori("keys", 8) as i:
            before = [DVE.now(), PE.now(), AC.now()]
            for j in range(2):
                t = now(h_unit(j))
                needs(sc, t, *before)
                a = lin_act[j].did(sc.activation(qT[j][:, :], lin[j][:, :], ACT.Copy))
                needs(te, a, t_keys, *before)
                for n in range(TT):
                    a = te.matmul(t_bank[j][:, n * P:(n + 1) * P], qT[j][:, n * P:(n + 1) * P],
                                  keysT[:, bass.ds(i * 2 + j, 1), :], start=True, stop=True)
                a = PE.did(a)
                needs(sc, a)
                a = AC.did(sc.activation(s_sb[j][:, :, :], t_bank[j][:, :].rearrange("p (n k) -> p n k", n=TT), ACT.Copy))
                for n in range(TT):
                    a = top16([two_v[:, n, j, 0:8], two_v[:, n, j, 8:16]], [two_i[:, n, j, 0:8], two_i[:, n, j, 8:16]],
                              s_sb[j][:, n, :], work[:, 0:P], [a, DVE.now()])
            needs(ve, a)
            DVE.did(ve.tensor_copy(vals[:, :, bass.ds(i * 2, 2), :], two_v[:, :, :, :]))
            DVE.did(ve.tensor_copy(index[:, :, bass.ds(i * 2, 2), :], two_i[:, :, :, :]))
        barrier()
        cand = sb(st, "cand", [P, H8, K16, K16])
        oh = sb(st, "oh", [P, H8, K16, K16])
        best = sb(st, "best", [P, H8, K16])
        pos = sb(st, "pos", [P, H8, K16], U32)
        part = sb(st, "part", [P, H8, K16], U32)
        partf = sb(st, "partf", [P, H8, K16])
        idxf = sb(st, "idxf", [P, H8, 2, K16])
        rs = sb(st, "prs", [P, H8])
        res = sb(st, "pres", [P, 3, P])
        table_set("exp_and_others")
        with pr.fori("combine", TT) as i:
            needs(ve, everything(), t_iota)
            mine = bass.ds(i, 1)
            v4 = vals[:, mine, :, :].rearrange("p a (h c) k -> p (a h) c k", c=2)
            first = v4[:, :, 0, :].unsqueeze(3).to_broadcast([P, H8, K16, K16])
            second = v4[:, :, 1, :].unsqueeze(2).to_broadcast([P, H8, K16, K16])
            a = DVE.did(ve.tensor_tensor(cand[:, :, :, :], first, second, ALU.add))
            DVE.did(ve.tensor_copy(idxf[:, :, :, :].rearrange("p h c k -> p (h c) k"), index[:, mine, :, :].rearrange("p a c k -> p (a c) k")))
            for h in range(H8):
                src = cand[:, h, :, :].rearrange("p a b -> p (a b)")
                a = top16([best[:, h, 0:8], best[:, h, 8:16]], [pos[:, h, 0:8], pos[:, h, 8:16]], src, work[:, :], [a, DVE.now()])
            needs(ve, a)
            g3 = res[:, 0, :].rearrange("p (h k) -> p h k", h=H8)
            c = DVE.did(ve.tensor_tensor(g3, best[:, :, :], best[:, :, 0:1].to_broadcast([P, H8, K16]), ALU.subtract))
            needs(sc, c)
            b = AC.did(sc.activation(res[:, 0, :], res[:, 0, :], ACT.Exp))
            needs(ve, b)
            c = DVE.did(ve.tensor_reduce(rs[:, :], g3, AX.X, ALU.add))
            needs(ve, c)
            c = DVE.did(ve.reciprocal(rs[:, :], rs[:, :]))
            needs(ve, c)
            c = DVE.did(ve.tensor_tensor(g3, g3, rs[:, :].unsqueeze(2).to_broadcast([P, H8, K16]), ALU.mult))
            for half in range(2):
                if half == 0:
                    c = DVE.did(ve.tensor_scalar(part[:, :, :], pos[:, :, :], 4, None, ALU.logical_shift_right))
                else:
                    c = DVE.did(ve.tensor_scalar(part[:, :, :], pos[:, :, :], 15, None, ALU.bitwise_and))
                needs(ve, c)
                c = DVE.did(ve.tensor_copy(partf[:, :, :], part[:, :, :]))
                needs(ve, c)
                o3 = oh[:, :, :, :].rearrange("p h k a -> p (h k) a")
                c = DVE.did(ve.tensor_tensor(o3, partf[:, :, :].rearrange("p h k -> p (h k)").unsqueeze(2).to_broadcast([P, HK, K16]),
                                             iota16[:, :].unsqueeze(1).to_broadcast([P, HK, K16]), ALU.is_equal))
                needs(ve, c)
                c = DVE.did(ve.tensor_tensor(oh[:, :, :, :], oh[:, :, :, :],
                                             idxf[:, :, half, :].unsqueeze(2).to_broadcast([P, H8, K16, K16]), ALU.mult))
                needs(ve, c)
                c = DVE.did(ve.tensor_reduce(res[:, 1 + half, :], o3, AX.X, ALU.add))
                needs(ve, c)
            needs(te, c)
            for n in range(3):
                a = te.transpose(t_bank[0][:, n * P:(n + 1) * P], res[:, n, :], ident[:, :])
            a = PE.did(a)
            needs(sc, a)
            for n, dst in enumerate((gT, iT, jT)):
                AC.did(sc.activation(dst[:, bass.ds(i * P, P)], t_bank[0][:, n * P:(n + 1) * P], ACT.Copy))

    def scatter(st, gT, iT, jT):
        iota = sb(st, "iota", [P, P])
        A = [sb(st, f"oneA{b}", [P, 4, P]) for b in range(4)]
        B = [sb(st, f"oneB{b}", [P, 4, P]) for b in range(4)]
        j_now = sb(st, "j_now", [P, 2 * G_TOK])
        G = [sb(st, f"G{b}", [P, HK, G_TOK]) for b in range(2)]
        banks = s_bank + t_bank
        out = [Counter(pr, f"G_dma{b}", 16) for b in range(2)]
        t_iota = [out[b].did(sc.dma_start(iota[:, b * DH:(b + 1) * DH], tabs("iota", P)[:, b * DH:(b + 1) * DH])) for b in range(2)]
        needs(ve, t_iota)
        needs(gp, t_iota)
        with pr.fori("scatter", G_BATCH // 2) as i:
            pe_t = [PE.now(3 - b) for b in range(4)]
            act_t = [AC.now(3 - b) for b in range(4)]
            pr.needs_first(gp, PO.now())
            b = PO.did(gp.tensor_copy(j_now[:, :], jT[:, bass.ds(i * 2 * G_TOK, 2 * G_TOK)]))
            pr.needs_first(gp, b)
            for half in range(2):
                needs(sc, out[half].now())
                for grp in range(4):
                    k = half * G_TOK + grp * 4
                    if grp % 2:
                        pr.needs_first(gp, pe_t[grp])
                        for n in range(4):
                            b = PO.did(gp.tensor_scalar(B[grp][:, n, :], iota[:, :], j_now[:, k + n:k + n + 1], None, ALU.is_equal))
                        needs(ve, pe_t[grp])
                    else:
                        needs(ve, pe_t[grp])
                        four = jT[:, bass.ds(i * 2 * G_TOK + k, 4)]
                        b = DVE.did(ve.tensor_tensor(B[grp][:, :, :], iota[:, :].unsqueeze(1).to_broadcast([P, 4, P]),
                                                     four.unsqueeze(2).to_broadcast([P, 4, P]), ALU.is_equal))
                    for n in range(4):
                        tok = bass.ds(i * 2 * G_TOK + (half * G_TOK + grp * 4 + n), 1)
                        a = DVE.did(ve.tensor_scalar(A[grp][:, n, :], iota[:, :], iT[:, tok], gT[:, tok], ALU.is_equal, ALU.mult))
                    needs(te, a, b, act_t[grp])
                    for n in range(4):
                        c = te.matmul(banks[grp][:, n * P:(n + 1) * P], B[grp][:, n, :], A[grp][:, n, :], start=True, stop=True)
                    pe_t[grp] = PE.did(c)
                    needs(sc, pe_t[grp])
                    act_t[grp] = AC.did(sc.activation(G[half][:, :, grp * 4:grp * 4 + 4],
                                                      banks[grp][:, :].rearrange("p (t i) -> p i t", t=4), ACT.Copy))
                needs(sc, act_t[3])
                out[half].did(sc.dma_start(g_dram[bass.ds(i * 2 + half, 1), :, :, :].rearrange("a p i t -> (a p) i t"), G[half][:, :, :]))
        state["g_written"] = [c.now() for c in out]

    def experts(st):
        Gin = sb(st, "Gin", [P, G_BATCH, H8, G_TOK])
        af = [sb(st, f"af{j}", [P, T]) for j in range(2)]
        e_hi = sb(st, "e_hi", [P, KT, T], F32R)
        e_lo = sb(st, "e_lo", [P, KT, T], F32R)
        g_in = Counter(pr, "G_in", 16)
        needs(gp, state["g_written"])

        def fetch_g(i, free):
            needs(gp, free)
            return g_in.did(gp.dma_start(Gin[:, :, :, :].rearrange("p b i t -> p b (i t)"),
                                         g_dram[:, :, bass.ds(i * H8, H8) if not isinstance(i, int) else slice(i * H8, (i + 1) * H8), :]
                                         .rearrange("b p i t -> p b (i t)")))

        def group(i, last):
            t_g = g_in.now()
            freed = [DVE.now(), DVE.now()]
            parts = []
            for j in range(KT):
                b = j % 2
                t = now(h_unit(b))
                needs(sc, t, freed[b])
                a = lin_act[b].did(sc.activation(af[b][:, :], lin[b][:, :], ACT.Gelu_apprx_tanh))
                needs(ve, a, t_g)
                c = DVE.did(ve.tensor_tensor(af[b][:, :].rearrange("p (b t) -> p b t", t=G_TOK),
                                             af[b][:, :].rearrange("p (b t) -> p b t", t=G_TOK), Gin[:, :, j, :], ALU.mult))
                freed[b] = split(e_hi[:, j, :], e_lo[:, j, :], af[b][:, :], c)
                parts.append(freed[b])
            if not last:
                fetch_g(i + 1, c)
            for n in range(KT):
                b = n % 2
                t = now(unit(b, [(slice(0, T), [(k, e_hi[:, k, :], e_lo[:, k, :], parts[k]) for k in range(KT)])]))
                needs(ve, t)
                a = lin_dve[b].did(ve.scalar_tensor_tensor(x[:, n, :], lin[b][:, :], mod[:, 5 * KT + n, 0:1], x[:, n, :], ALU.mult, ALU.add))
                if last:
                    add_squares(n, x[:, n, :], a)

        fetch_g(0, everything())
        table_set("gelu_apprx_tanh_and_others")
        with pr.fori("experts", PEER_GROUPS - 1) as i:
            group(i, False)
        clear_squares()
        group(PEER_GROUPS - 1, True)

    state = {}

    def gain_of(name, off=0):
        return lambda k: col(name, off + k)

    for b in range(2):
        lin_dve[b].did(ve.memset(scaled_g[:, b, :], 0.0))
    split_weights()
    norm(x, T, gain_of("attn_norm"), None, h_hi, h_lo, t_x, False)
    even_phase()
    norm(x, T, gain_of("ffn_norm"), None, h_hi, h_lo)
    ffn_phase(0)
    norm(x, T, gain_of("attn_norm", KT), None, h_hi, h_lo)
    odd_phase()
    norm(x, T, gain_of("ffn_norm", KT), None, h_hi, h_lo)
    ffn_phase(1)
    norm_plain(gain_of("final_norm"), True)

    norm(x, T, lambda k: scaled_g[:, 0, k:k + 1], lambda k: mod[:, k, 0:1], h_hi, h_lo)
    with ExitStack() as st:
        ya = [sb(st, f"ya{p}", [P, CT, T], F32R) for p in range(2)]
        yb = [sb(st, f"yb{p}", [P, CT, T], F32R) for p in range(2)]
        with ExitStack() as s2:
            neighbour_phase(s2, *ya)
        with ExitStack() as s2:
            gating_phase(s2, *yb)
        with ExitStack() as s2:
            m_hi, m_lo = (sb(s2, f"m_part{p}", [P, KT, T], F32R) for p in range(2))
            merge_phase(s2, *ya, *yb, m_hi, m_lo)
            out_proj("out2", m_hi, m_lo, lambda n: mod_flat[:, bass.ds(n * 2 + 4 * KT, 1)])
            barrier()
    norm(x, T, lambda k: scaled_g[:, 2, k:k + 1], lambda k: mod[:, 3 * KT + k, 0:1], h_hi, h_lo)
    peer_phase()
    norm_plain(gain_of("final_g"), False)
    y_out = Counter(pr, "y_out", 16)
    needs(sc, everything())
    t = y_out.did(sc.dma_start(io["out"], x[:, :, :]))
    needs(sc, t)
    assert used.n == n_units == lo_done.n, (used.n, n_units, lo_done.n)
    pr.stack.close()
    return pr.found


def units_of(w, blocks=KT):
    k, n = w.shape
    return w.reshape(blocks, P, n // P, P).transpose(2, 1, 0, 3).reshape(n // P, P, blocks * P)


def padded(w, n=P):
    out = np.zeros((w.shape[0], n), w.dtype)
    out[:, :w.shape[1]] = w
    return out


def by_tile(v):
    return v.reshape(-1, P).T


def tables():
    t = np.zeros((P, N_TABS), np.float32)

    def put(name, a):
        t[:a.shape[0], TABS[name]:TABS[name] + a.shape[1]] = a

    inv = np.float32(500000.0) ** (-(np.arange(8, dtype=np.float32) * np.float32(2.0) / np.float32(16)))
    for c, s, pos in (("cos", "sin", np.arange(T)), ("cos_cmp", "sin_cmp", np.arange(N_CMP) * 16 + CMP_LEN - 1)):
        ang = (pos.astype(np.float32)[None, :] * inv[:, None]).astype(np.float32).astype(np.float64)
        cos, sin = np.ones((P, len(pos))), np.zeros((P, len(pos)))
        for base in (0, DH):
            for half in (0, 8):
                cos[base + half:base + half + 8] = np.cos(ang)
                sin[base + half:base + half + 8] = np.sin(ang)
        put(c, cos.astype(np.float32))
        put(s, sin.astype(np.float32))
    perm = np.zeros((P, P), np.float32)
    for base in (0, DH):
        for d in range(8):
            perm[base + 8 + d, base + d] = -1.0
            perm[base + d, base + 8 + d] = 1.0
    put("perm", perm)
    put("ident", np.eye(P, dtype=np.float32))
    r = np.arange(P)
    put("causal_neg", np.where(r[None, :] <= r[:, None], 0.0, NEG).astype(np.float32))
    put("strict_t", (r[:, None] < r[None, :]).astype(np.float32))
    put("tri", (r[:, None] > r[None, :]).astype(np.float32))
    c = np.arange(DH)
    start = np.clip(c - 8, 0, DH - 16)
    win = np.where((c[None, :] >= start[:, None]) & (c[None, :] < start[:, None] + 16), 0.0, NEG).astype(np.float32)
    put("win_neg", np.concatenate([win, win]))
    tok = np.arange(T).reshape(TT, P)
    end = np.arange(32) * 16 + CMP_LEN - 1
    cm = np.where(end[None, None, :] <= tok[:, :, None], 0.0, NEG).astype(np.float32)
    put("cmp_neg", cm.transpose(1, 0, 2).reshape(P, TT * 32))
    put("iota", np.broadcast_to(np.arange(P, dtype=np.float32), (P, P)))
    put("iota16", np.broadcast_to(np.arange(16, dtype=np.float32), (P, 16)))
    return t


def layout(a):
    ev = a["ev_w_in"][0]
    off = np.cumsum([0, 512, 512, 512, 512, 128, 128, 128, 128, 128, 128, 24])
    seg = [ev[:, off[n]:off[n + 1]] for n in range(11)]
    sq, sk, sv, nq, kc, vc, ksl, vsl, kwn, vwn, gate = seg
    head = lambda w, h: w[:, h * DH:(h + 1) * DH]
    pair = lambda w, p: w[:, p * P:(p + 1) * P]
    small = [padded(gate), kc, vc, ksl, kwn, vsl, vwn]
    small += [np.concatenate([head(nq, p), head(nq, p + 4)], 1) for p in range(4)]
    small += [pair(w, p) for p in range(4) for w in (sq, sk, sv)]
    u8 = [units_of(w) for w in small]
    wo = a["ev_w_out"][0]
    rows = [wo[0:512]] + [wo[512 + h * DH:512 + (h + 1) * DH] for p in range(4) for h in (p, p + 4)]
    u8.append(units_of(np.concatenate(rows)))
    u11 = []
    for layer in range(2):
        if layer == 1:
            od = a["od_w_in"][0]
            f = od[:, 3072:3088]
            u8.append(units_of(np.concatenate([padded(f, DH), padded(f, DH)], 1)))
            u8 += [units_of(pair(od[:, 1024 * n:1024 * (n + 1)], p)) for p in range(8) for n in range(3)]
            u8.append(units_of(a["od_w_out"][0]))
        w = units_of(a["ffn_w_in"][layer]).reshape(2, FFT, P, D)
        u8.append(w.transpose(1, 0, 2, 3).reshape(2 * FFT, P, D))
        w = a["ffn_w_out"][layer]
        u11 += [units_of(w[h * FFH * P:(h + 1) * FFH * P], FFH) for h in range(2)]
    w = a["w_in_2"][0]
    u8 += [units_of(pair(w[:, 512 * n:512 * (n + 1)], p)) for p in range(4) for n in range(3)]
    u8 += [units_of(w[:, 2048:2560]), units_of(w[:, 1536:2048])]
    pab = np.concatenate([a["w_proj_a_2"][0], a["w_proj_b_2"][0]])
    three = np.stack([units_of(w[:, 2560:3584]), units_of(w[:, 3584:4608]), units_of(pab)], 1)
    u8.append(three.reshape(24, P, D))
    u8.append(units_of(a["w_out_2"][0]))
    u8.append(units_of(a["peer_wq_2"][0]))
    U = a["peer_u_2"][0].reshape(PEER_GROUPS, 8, P, KT, P).transpose(0, 1, 4, 3, 2).reshape(PEER_GROUPS, 8, P, D)
    V = a["peer_v_2"][0].reshape(PEER_GROUPS, 8, P, KT, P).transpose(0, 3, 2, 1, 4).reshape(PEER_GROUPS, 8, P, D)
    u8.append(np.concatenate([U, V], 1).reshape(PEER_GROUPS * 16, P, D))
    ada = a["ada_w_2"][0].reshape(KT, P, -1, 256).transpose(2, 1, 0, 3)
    out = {"ada_w": ada, "w8": np.concatenate(u8), "w11": np.concatenate(u11), "tabs": tables()}
    to_tiles = lambda m: m.T.reshape(KT, P, -1).transpose(1, 0, 2)
    out["x"] = to_tiles(a["x"][0])
    out["ctx"] = to_tiles(a["ctx_2"][0])
    cols = np.zeros((P, N_COLS), np.float32)

    def put(name, m):
        cols[:, COLS[name]:COLS[name] + m.shape[1]] = m

    for name, key in (("attn_norm", "attn_norm"), ("ffn_norm", "ffn_norm"), ("final_norm", "final_norm"), ("norm1", "norm1_g_2"),
                      ("norm2", "norm2_g_2"), ("final_g", "final_g_2"), ("conv_w", "ffn_conv_w"), ("conv_b", "ffn_conv_b"),
                      ("ada_b", "ada_b_2"), ("ln_g", "gm_ln_g_2")):
        put(name, by_tile(np.ascontiguousarray(a[key]).reshape(-1)))
    bf = np.zeros((P, 1), np.float32)
    bf[0:16, 0] = bf[DH:DH + 16, 0] = a["od_b_f"][0]
    put("b_f", bf)
    put("c", np.stack([by_tile(a["c_2"].reshape(-1)), by_tile(a["c_ctx_2"])], 2).reshape(P, 16))
    for name, key in (("pe_k", "ev_cmp_pos_k"), ("pe_v", "ev_cmp_pos_v")):
        put(name, np.concatenate([a[key][0].T, a[key][0].T]))
    out["cols"] = cols
    cw = np.zeros((2, P, CMP_LEN, P), np.float32)
    for n, key in enumerate(("ev_cmp_w_k", "ev_cmp_w_v")):
        w = a[key][0].reshape(CMP_LEN, DH, DH).transpose(1, 0, 2)
        cw[n, 0:DH, :, 0:DH] = w
        cw[n, DH:, :, DH:] = w
    out["cmp_w"] = cw
    rpb = a["na_rpb_2"][0]
    c = np.arange(DH)
    dc = np.clip(c[None, :] - c[:, None] + 15, 0, 30)
    e = np.arange(1, 15)
    b = np.stack([rpb[:, (e - r)[:, None, None], dc[None]] for r in range(2)], 1)
    out["bias"] = b.transpose(0, 1, 3, 2, 4).reshape(4, 2, P, 14, DH).transpose(0, 2, 1, 3, 4).reshape(4, P, 28 * DH)
    out["ws"] = a["gm_ws_2"][0].transpose(2, 0, 1)
    out["bs"] = np.repeat(a["gm_bs_2"][0].reshape(4, 2, 1, P), DH, axis=2).reshape(4, P, P).transpose(1, 0, 2)
    out["keys"] = a["peer_keys_2"][0].reshape(16, P, P).transpose(2, 0, 1)
    return {k: np.ascontiguousarray(v) for k, v in out.items()}


def build(nc, shapes, deltas):
    io = {n: nc.dram_tensor(f"in_{n}", v, F32, kind="ExternalInput").ap() for n, v in shapes.items()}
    io["out"] = nc.dram_tensor("out_y", (P, KT, T), F32, kind="ExternalOutput").ap()
    return program(nc, io, deltas)


def kernel(**inputs):
    from concourse import bacc
    from concourse.bass_utils import run_bass_kernel_spmd
    arrays = layout({k: np.asarray(v) for k, v in inputs.items()})
    shapes = {k: v.shape for k, v in arrays.items()}
    deltas = {}
    for _ in range(2):
        nc = bacc.Bacc("TRN2", target_bir_lowering=False, num_devices=1)
        deltas = build(nc, shapes, deltas)
    r = run_bass_kernel_spmd(nc, [{f"in_{k}": v for k, v in arrays.items()}], core_ids=[0])
    y = r.results[0]["out_y"]
    return np.ascontiguousarray(y.transpose(2, 1, 0).reshape(1, T, D))
```

```python
from contextlib import ExitStack, contextmanager

import numpy as np

import concourse.bass as bass
from concourse import mybir

F32 = mybir.dt.float32
F32R = mybir.dt.float32r
BF16 = mybir.dt.bfloat16
U32 = mybir.dt.uint32
ALU = mybir.AluOpType
ACT = mybir.ActivationFunctionType
AX = mybir.AxisListType

P = 128
D = 1024
KT = D // P
T = 512
TT = T // P
DH = 64
FF = 2816
FFT = FF // P
FFH = FFT // 2
N_CMP = 31
CMP_LEN = 32
CTX = 256
CTT = CTX // P
N_ADA = 6 * KT
HK = 128
PEER_GROUPS = 16
AHEAD = 5
TOK_BATCH = 32
N_BATCH = T // TOK_BATCH
SCALE = 0.125
NEG = -1e30
EPS = 1e-6

COLS = {}
_at = 0
for _name, _n in (("attn_norm", 16), ("ffn_norm", 16), ("final_norm", 8), ("norm1", 8), ("norm2", 8),
                  ("final_g", 8), ("conv_w", 2 * 3 * FFT), ("conv_b", 2 * FFT), ("b_f", 1), ("ada_b", N_ADA),
                  ("ln_g", 4), ("c", 16), ("pe_k", CMP_LEN), ("pe_v", CMP_LEN)):
    COLS[_name] = _at
    _at += _n
N_COLS = _at

TABS = {}
_at = 0
for _name, _n in (("cos", T), ("sin", T), ("cos_cmp", 32), ("sin_cmp", 32), ("perm", P), ("ident", P),
                  ("causal_neg", P), ("strict_t", P), ("tri", P), ("win_neg", DH), ("cmp_neg", TT * 32),
                  ("iota", P), ("iota16", 16)):
    TABS[_name] = _at
    _at += _n
N_TABS = _at


class Loop:
    def __init__(self, i, name, deltas):
        self.i, self.name, self.deltas = i, name, deltas


class Ticket:

    def __init__(self, sem, value, coef=0, loop=None):
        self.sem, self.value, self.coef, self.loop = sem, value, coef, loop


class Program:

    def __init__(self, nc, deltas):
        self.nc, self.deltas, self.found = nc, deltas, {}
        self.loop = None
        self.counters = []
        self.stack = ExitStack()
        self.waited = {}
        self.gates = {e.engine: self.stack.enter_context(nc.semaphore(n)) for n, e in (("dve_gate", nc.vector), ("pool_gate", nc.gpsimd))}
        self.pe, self.dve, self.act, self.pool = (Counter(self, n) for n in ("pe_done", "dve_done", "act_done", "pool_done"))

    def needs(self, engine, *tickets):
        for t in tickets:
            if t is None:
                continue
            if isinstance(t, (list, tuple)):
                self.needs(engine, *t)
                continue
            assert t.loop is None or t.loop is self.loop, "a ticket of a loop that has ended"
            if t.value <= 0 and t.coef == 0:
                continue
            key = (engine.engine, t.sem, t.loop.name if t.loop else None)
            assert t.value > 0, "a wait on a register's value has to be positive from the first pass on"
            if self.waited.get(key, 0) >= t.value:
                continue
            self.waited[key] = t.value
            engine.wait_ge(t.sem, t.value + t.loop.i * t.coef if t.loop and t.coef else t.value)

    def needs_first(self, engine, *tickets):
        self.needs(engine, *tickets)
        if self.loop:
            engine.sem_inc(self.gates[engine.engine], 1)

    @contextmanager
    def fori(self, name, n):
        start = [(c, c.n) for c in self.counters]
        deltas = self.deltas.get(name, {})
        self.waited = {}
        with self.nc.Fori(0, n) as i:
            self.loop = Loop(i, name, deltas)
            yield i
        self.found[name] = {c.name: c.n - s for c, s in start}
        self.loop = None
        self.waited = {}
        for c, s in start:
            c.n = s + n * (c.n - s)

    def delta(self, name):
        return self.loop.deltas.get(name, 0) if self.loop else 0


class Counter:

    def __init__(self, prog, name, step=1):
        self.prog, self.name, self.step, self.n = prog, name, step, 0
        self.sem = prog.stack.enter_context(prog.nc.semaphore(name))
        prog.counters.append(self)

    def did(self, ins):
        self.n += 1
        ins.then_inc(self.sem, self.step)
        return self.now()

    def now(self, back=0):
        p = self.prog
        return Ticket(self.sem, (self.n - back) * self.step, p.delta(self.name) * self.step, p.loop)


def run_together(*gens):
    live = [[g, k] for g, k in gens]
    while live:
        for entry in list(live):
            for _ in range(entry[1]):
                try:
                    next(entry[0])
                except StopIteration:
                    live.remove(entry)
                    break


def program(nc, io, deltas):
    pr = Program(nc, deltas)
    top = pr.stack
    needs, PE, DVE, AC, PO = pr.needs, pr.pe, pr.dve, pr.act, pr.pool
    te, ve, sc, gp, sy = nc.tensor, nc.vector, nc.scalar, nc.gpsimd, nc.sync

    def sb(stack, name, shape, dt=F32):
        return stack.enter_context(nc.sbuf_tensor(name, shape, dt))

    bank = [top.enter_context(nc.psum_tensor(f"bank{b}", [P, 512], F32)) for b in range(8)]
    lin = bank[0:2]
    s_bank, t_bank, o_bank, x_bank = bank[2:4], bank[4:6], bank[6], bank[7]
    WMAX = FFH * P
    w_raw = [sb(top, f"w_raw{s}", [P, WMAX]) for s in range(2)]
    w_hi = [sb(top, f"w_hi{s}", [P, WMAX], F32R) for s in range(2)]
    w_lo = [sb(top, f"w_lo{s}", [P, WMAX], F32R) for s in range(2)]
    x = sb(top, "x", [P, KT, T])
    h_hi = sb(top, "h_hi", [P, KT, T], F32R)
    h_lo = sb(top, "h_lo", [P, KT, T], F32R)
    cols = sb(top, "cols", [P, N_COLS])
    ident = sb(top, "ident", [P, P])
    ones = sb(top, "ones", [P, P])
    mod = sb(top, "mod", [P, N_ADA, 2])
    scaled_g = sb(top, "scaled_g", [P, 3, KT])

    w_in = [top.enter_context(nc.semaphore(f"weights_in{s}")) for s in range(2)]
    hi_done = Counter(pr, "weights_hi")
    lo_done = Counter(pr, "weights_lo")
    used = Counter(pr, "weights_used")
    plan = [("w8", 11 + 12 + 8)]
    for _ in range(2):
        plan += [("w8", 22), ("w11", 8), ("w8", 22), ("w11", 8)]
        if _ == 0:
            plan += [("w8", 1 + 24 + 8)]
    plan += [("w8", 12 + 8 + 24 + 8 + 16 + 256)]
    n_units = sum(n for _, n in plan)

    def load_weights():
        unit, at = 0, {"w8": 0, "w11": 0}

        def fetch(src, k, unit_base, row, after):
            slot = (unit_base + k) % 2
            if after is not None:
                sy.wait_ge(lo_done.sem, after)
            n = io[src].shape[2]
            sy.dma_start(w_raw[slot][:, 0:n], io[src][row, :, :].rearrange("a p n -> p (a n)") if not isinstance(row, int)
                         else io[src][row]).then_inc(w_in[slot], 16)

        for src, n in plan:
            done = 0
            while done < n and unit < 2:
                fetch(src, 0, unit, at[src], None)
                unit, done, at[src] = unit + 1, done + 1, at[src] + 1
            pairs = (n - done) // 2
            if pairs > 1:
                with sy.Fori(0, pairs) as j:
                    for k in range(2):
                        fetch(src, k, unit, bass.ds(j * 2 + (at[src] + k), 1), j * 2 + (unit + k - 1))
                unit, done, at[src] = unit + 2 * pairs, done + 2 * pairs, at[src] + 2 * pairs
            while done < n:
                fetch(src, 0, unit, at[src], unit - 1)
                unit, done, at[src] = unit + 1, done + 1, at[src] + 1

    def split_hi(blocks=KT):
        u = lo_done.n
        if pr.loop is None and u >= n_units:
            return
        slot, n = u % 2, blocks * P
        d = pr.delta("weights_lo")
        arrived = Ticket(w_in[slot], 16 * (u // 2 + 1), 8 * d, pr.loop)
        free = Ticket(used.sem, u - 1, d, pr.loop)
        needs(sc, arrived, free)
        hi = hi_done.did(sc.activation(w_hi[slot][:, 0:n], w_raw[slot][:, 0:n], ACT.Copy))
        return slot, n, [arrived, free, hi]

    def split_lo(parts):
        if parts:
            slot, n, ready = parts
            needs(ve, *ready)
            lo_done.did(ve.tensor_tensor(w_lo[slot][:, 0:n], w_raw[slot][:, 0:n], w_hi[slot][:, 0:n], ALU.subtract))

    def split_weights(blocks=KT):
        split_lo(split_hi(blocks))

    lin_act = [Counter(pr, f"bank{b}_read_by_act") for b in range(2)]
    lin_dve = [Counter(pr, f"bank{b}_read_by_dve") for b in range(2)]

    def unit(b, groups, then=KT, before=(), late=False):
        u = used.n
        slot = u % 2
        if not late:
            split_weights(then)
        needs(te, Ticket(lo_done.sem, u + 1, pr.delta("weights_lo"), pr.loop), lin_act[b].now(), lin_dve[b].now(), *before)
        last = None
        for at, (columns, blocks) in enumerate(groups):
            out = lin[b][:, columns] if isinstance(columns, slice) else columns
            for k, (w, hi, lo, *ready) in enumerate(blocks):
                needs(te, ready)
                wh, wl = w_hi[slot][:, w * P:(w + 1) * P], w_lo[slot][:, w * P:(w + 1) * P]
                te.matmul(out, wh, hi, start=(k == 0), stop=False)
                te.matmul(out, wh, lo, start=False, stop=False)
                last = te.matmul(out, wl, hi, start=False, stop=(k == len(blocks) - 1))
                if late and at == 0 and k == 1:
                    parts = split_hi(then)
                if late and at == 0 and k == 7:
                    split_lo(parts)
                if k % 2:
                    yield
        return used.did(last)

    def h_unit(b, **kw):
        return unit(b, [(slice(0, T), [(k, h_hi[:, k, :], h_lo[:, k, :], h_ready[k]) for k in range(KT)])], **kw)

    def now(gen):
        while True:
            try:
                next(gen)
            except StopIteration as e:
                return e.value

    def everything():
        return [c.now() for c in (PE, DVE, AC, PO, used, lo_done, hi_done, *lin_act, *lin_dve)]

    def all_but_pe():
        return [c.now() for c in (DVE, AC, PO, *lin_act, *lin_dve)]

    def barrier():
        t = everything()
        for e in (te, ve, sc, gp):
            needs(e, t)

    def split(hi, lo, src, *before):
        needs(sc, *before)
        a = AC.did(sc.activation(hi, src, ACT.Copy))
        needs(ve, *before)
        needs(ve, a)
        return DVE.did(ve.tensor_tensor(lo, src, hi, ALU.subtract))

    def col(name, k=0, n=1):
        return cols[:, COLS[name] + k:COLS[name] + k + n]

    def table_set(name):
        sc.preload_act_table_set(name)

    def dma_in(name, dst, src, engine=None):
        c = Counter(pr, name, 16)
        return c.did((engine or sc).dma_start(dst, src))

    load_weights()
    t_cols = dma_in("cols_in", cols[:, :], io["cols"])
    tabs = lambda name, n=None: io["tabs"][:, TABS[name]:TABS[name] + n]
    t_ident = dma_in("ident_in", ident[:, :], tabs("ident", P))
    t_x = dma_in("x_in", x[:, :, :], io["x"])
    t_ones = PO.did(gp.memset(ones[:, :], 1.0))

    acc = sb(top, "acc", [P, T])
    nv = sb(top, "norm_v", [P, T])
    ny = sb(top, "norm_y", [P, T])
    hf = [sb(top, f"norm_h{s}", [P, T]) for s in range(2)]
    h_ready = []

    def rstd_of(sums, n, denom, ready):
        v, y, t1 = nv[:, 0:n], ny[:, 0:n], acc[:, 0:n]
        needs(ve, ready)
        a = DVE.did(ve.tensor_scalar(v, sums, 1.0 / denom, EPS, ALU.mult, ALU.add))
        needs(ve, a)
        a = DVE.did(ve.reciprocal(t1, v))
        needs(sc, a)
        b = AC.did(sc.activation(y, t1, ACT.Sqrt))
        needs(ve, b)
        a = DVE.did(ve.tensor_tensor(t1, y, y, ALU.mult))
        needs(ve, a)
        a = DVE.did(ve.scalar_tensor_tensor(t1, v, -0.5, t1, ALU.mult, ALU.mult))
        needs(ve, a)
        return DVE.did(ve.scalar_tensor_tensor(y, t1, 1.5, y, ALU.add, ALU.mult))

    def clear_squares():
        pr.needs_first(gp, DVE.now(), PE.now(), AC.now())
        PO.did(gp.memset(acc[:, :], 0.0))

    def add_squares(k, src, t):
        needs(sc, t, PO.now(1))
        a = AC.did(sc.activation(hf[k % 2][:, :], src, ACT.Square))
        pr.needs_first(gp, a, PO.now())
        PO.did(gp.tensor_tensor(acc[:, :], acc[:, :], hf[k % 2][:, :], ALU.add))

    def total(out, n):
        needs(te, PO.now(), t_ones)
        return PE.did(te.matmul(out, ones[:, :], acc[:, 0:n], start=True, stop=True))

    def column_sums(src, tiles, n, out, square, ready):
        freed = [None, None]
        for k in range(tiles):
            if square:
                needs(sc, ready, freed[k % 2])
                a = AC.did(sc.activation(hf[k % 2][:, 0:n], src[:, k, :], ACT.Square))
                needs(te, a)
            else:
                needs(te, ready)
            moving = hf[k % 2][:, 0:n] if square else src[:, k, :]
            freed[k % 2] = PE.did(te.matmul(out, ones[:, :], moving, start=(k == 0), stop=(k == tiles - 1)))
        return freed[(tiles - 1) % 2]

    def norm(src, n, gain, shift, hi, lo, ready=None, have_squares=True):
        barrier()
        table_set("sqrt_and_others")
        out = bank[2][:, 0:n]
        s = total(out, n) if have_squares else column_sums(src, KT, n, out, True, ready)
        r = rstd_of(out, n, D, s)
        done, half = [], []
        for k in range(KT + 1):
            if k < KT:
                needs(ve, r, s, done[k - 2] if k >= 2 else None)
                t = DVE.did(ve.scalar_tensor_tensor(hf[k % 2][:, 0:n], src[:, k, :], gain(k), ny[:, 0:n], ALU.mult, ALU.mult))
                needs(sc, t)
                if shift is not None:
                    t = AC.did(sc.activation(hf[k % 2][:, 0:n], hf[k % 2][:, 0:n], ACT.Identity, bias=shift(k)))
                    needs(sc, t)
                half.append(AC.did(sc.activation(hi[:, k, :], hf[k % 2][:, 0:n], ACT.Copy)))
            if k:
                needs(ve, half[k - 1])
                done.append(DVE.did(ve.tensor_tensor(lo[:, k - 1, :], hf[(k - 1) % 2][:, 0:n], hi[:, k - 1, :], ALU.subtract)))
        if hi is h_hi:
            h_ready[:] = done
        return done

    def norm_plain(gain, squares):
        barrier()
        r = rstd_of(bank[2][:, :], T, D, total(bank[2][:, :], T))
        if squares:
            clear_squares()
        for k in range(KT):
            needs(ve, r)
            a = DVE.did(ve.scalar_tensor_tensor(x[:, k, :], x[:, k, :], gain(k), ny[:, :], ALU.mult, ALU.mult))
            if squares:
                add_squares(k, x[:, k, :], a)
            elif k % 2:
                needs(sc, a)
                y_out.did(sc.dma_start(io["out"][:, k - 1:k + 1, :], x[:, k - 1:k + 1, :]))

    ADA_STEP = 2
    ADA_STEPS = N_ADA // ADA_STEP // 2
    ADA_COLS = ADA_STEP * P

    def ada_units(st):
        silu = sb(st, "silu_c", [P, KT, 2])
        rows = sb(st, "ada_rows", [2, ADA_COLS])
        slot = [sb(st, f"ada_w{b}", [P, KT, ADA_COLS]) for b in range(2)]
        arrived = [Counter(pr, f"ada_in{b}", 16) for b in range(2)]
        needs(sc, t_cols)
        t_silu = AC.did(sc.activation(silu[:, :, :], col("c", 0, 16).rearrange("p (k c) -> p k c", c=2), ACT.Silu))

        def fetch(i, k, free):
            pr.needs_first(gp, free)
            arrived[k % 2].did(gp.dma_start(slot[k % 2][:, :, :], io["ada_w"][bass.ds(i * ADA_STEPS + k, 1), :, :, :]
                                            .rearrange("a p u n -> (a p) u n")))

        def steps(i, entry):
            for k in range(2):
                fetch(i, k, entry)
            read = entry
            for k in range(ADA_STEPS):
                needs(te, arrived[k % 2].now(), t_silu, read)
                for c in range(KT):
                    a = te.matmul(x_bank[0:2, 0:ADA_COLS], silu[:, c, :], slot[k % 2][:, c, :], start=(c == 0), stop=(c == KT - 1))
                    if c == KT - 1:
                        a = PE.did(a)
                    if c % 3 == 1:
                        yield
                if k + 2 < ADA_STEPS:
                    fetch(i, k + 2, a)
                needs(ve, a)
                b = DVE.did(ve.tensor_copy(rows[:, :], x_bank[0:2, 0:ADA_COLS]))
                yield
                needs(te, b, t_ident)
                for n in range(ADA_STEP):
                    a = te.matmul(x_bank[:, ADA_COLS + 2 * n:ADA_COLS + 2 * n + 2], rows[:, n * P:(n + 1) * P], ident[0:2, 0:2], start=True, stop=True)
                a = PE.did(a)
                yield
                needs(ve, a, t_cols)
                at = i * (N_ADA // 2) + k * ADA_STEP
                bias = cols[:, bass.ds(at + COLS["ada_b"], ADA_STEP)].unsqueeze(2).to_broadcast([P, ADA_STEP, 2])
                read = DVE.did(ve.tensor_tensor(mod[:, bass.ds(at, ADA_STEP), :],
                                                x_bank[:, ADA_COLS:ADA_COLS + 2 * ADA_STEP].rearrange("p (n c) -> p n c", c=2), bias, ALU.add))
        return steps

    def modulated_gains():
        needs(ve, everything())
        for row, (chunk, c, g) in enumerate(((1, 0, "norm1"), (1, 1, "norm1"), (4, 0, "norm2"))):
            DVE.did(ve.scalar_tensor_tensor(scaled_g[:, row, :], mod[:, chunk * KT:(chunk + 1) * KT, c], 1.0,
                                            col(g, 0, KT), ALU.add, ALU.mult))

    def out_units(i, hi, lo, gain=None, blocks=KT, thens=(KT, KT), squares=True, ready=None):
        for j in range(2):
            t = now(unit(j, [(slice(0, T), [(k, hi[:, k, :], lo[:, k, :], ready and ready[k]) for k in range(blocks)])], then=thens[j]))
            xs = x[:, bass.ds(i * 2 + j, 1), :]
            needs(ve, t)
            if gain is None:
                a = lin_dve[j].did(ve.tensor_tensor(xs, lin[j][:, :], xs, ALU.add))
            else:
                a = lin_dve[j].did(ve.scalar_tensor_tensor(xs, lin[j][:, :], gain(i * 2 + j), xs, ALU.mult, ALU.add))
            if squares:
                add_squares(j, xs, a)

    def out_proj(name, hi, lo, gain=None):
        clear_squares()
        with pr.fori(name, KT // 2) as i:
            out_units(i, hi, lo, gain)

    def to_natural(vT, v_nat, s, tiles, ready, freed, reader=None):
        needs(te, ready, freed, t_ident)
        for j in range(tiles):
            a = te.transpose(s[:, j * P:(j + 1) * P], vT[:, j * P:(j + 1) * P], ident[:, :])
        a = PE.did(a)
        needs(sc, a)
        return (reader or AC).did(sc.activation(v_nat, s[:, 0:tiles * P].rearrange("p (j d) -> p j d", j=tiles), ACT.Copy))

    def softmax_rows(S, Pm, width, small, k, scale, ready, guard=False, gate=None):
        mx, nm, rs, rc = (small[:, 4 * k + c:4 * k + c + 1] for c in range(4))
        needs(ve, ready)
        a = DVE.did(ve.tensor_reduce(mx, S, AX.X, ALU.max))
        needs(ve, a)
        a = DVE.did(ve.tensor_scalar(nm, mx, -1e20 if guard else -3e38, -scale, ALU.max, ALU.mult))
        needs(sc, a)
        read = a = AC.did(sc.activation(Pm, S, ACT.Exp, bias=nm, scale=scale, accum_out=rs))
        yield
        needs(ve, a)
        if guard:
            a = DVE.did(ve.tensor_scalar(rs, rs, 1e-30, None, ALU.max))
            needs(ve, a)
        a = DVE.did(ve.reciprocal(rc, rs))
        needs(ve, a)
        if gate is not None:
            a = DVE.did(ve.tensor_tensor(rc, rc, gate, ALU.mult))
            needs(ve, a)
        return DVE.did(ve.tensor_scalar(Pm, Pm, rc, None, ALU.mult)), read

    def even_phase():
        with ExitStack() as st:
            o_hi = sb(st, "o_hi", [P, KT, T], F32R)
            o_lo = sb(st, "o_lo", [P, KT, T], F32R)
            with ExitStack() as s2:
                nsa_phase(s2, o_hi, o_lo)
                barrier()
            with ExitStack() as s2:
                stick_phase(s2, o_hi, o_lo)
                barrier()
                modulated_gains()
            out_proj("ev_out", o_hi, o_lo)
            barrier()

    def nsa_phase(st, o_hi, o_lo):
        tab = sb(st, "rope_tab", [P, 2 * T + 64 + P])
        t_tab = dma_in("rope_in", tab[:, :], io["tabs"][:, TABS["cos"]:TABS["cos"] + 2 * T + 64 + P])
        cos, sin = tab[:, 0:T], tab[:, T:2 * T]
        cos_c, sin_c, perm = tab[:, 2 * T:2 * T + 32], tab[:, 2 * T + 32:2 * T + 64], tab[:, 2 * T + 64:]
        neg = sb(st, "nsa_neg", [P, P])
        t_neg = dma_in("nsa_neg_in", neg[:, :], tabs("causal_neg", P))
        cneg = sb(st, "cmp_neg", [P, TT, 32])
        t_cneg = dma_in("cmp_neg_in", cneg[:, :, :], tabs("cmp_neg", TT * 32).rearrange("p (t c) -> p t c", t=TT))
        gates = sb(st, "gates", [P, TT, 24])
        kc = sb(st, "kc", [P, 32])
        vc = sb(st, "vc", [32, P])
        keys = [sb(st, f"k_branch{b}", [P, T]) for b in range(2)]
        vals = [sb(st, f"v_branch{b}", [P, TT, P]) for b in range(2)]
        raw = sb(st, "nsa_raw", [P, T])
        ta = sb(st, "rope_a", [P, T])
        tb = sb(st, "rope_b", [P, T])

        def rope(dst, src, n, c, s, scratch, r, freed, reader=None):
            needs(te, r, t_tab, freed)
            a = PE.did(te.matmul(scratch, perm, src, start=True, stop=True))
            needs(ve, r, t_tab, DVE.now())
            b = DVE.did(ve.tensor_tensor(ta[:, 0:n], src, c, ALU.mult))
            needs(ve, a)
            d = (reader or DVE).did(ve.tensor_tensor(tb[:, 0:n], scratch, s, ALU.mult))
            needs(ve, b, d)
            return DVE.did(ve.tensor_tensor(dst, ta[:, 0:n], tb[:, 0:n], ALU.add))

        with ExitStack() as cs:
            cw = sb(cs, "cmp_w", [P, CMP_LEN, P])
            blk = sb(cs, "cmp_blocks", [P, CMP_LEN, 32])
            names = ("gates", "k_cmp", "v_cmp", "k_sel", "k_win", "v_sel", "v_win")
            made = {n: sb(cs, f"made_{n}", [24 if n == "gates" else P, T]) for n in names}
            got = {}
            k_rows = sb(cs, "k_cmp_rows", [32, P])
            k_cols = sb(cs, "k_cmp_cols", [P, 32])

            def projections():
                for n in names:
                    b = used.n % 2
                    t = yield from h_unit(b)
                    needs(sc, t)
                    src = lin[b][0:24, :] if n == "gates" else lin[b][:, :]
                    got[n] = lin_act[b].did(sc.activation(made[n][:, :], src, ACT.Sigmoid if n == "gates" else ACT.Copy))
                    yield

            def arrived(n):
                while n not in got:
                    yield

            def derived():
                w_ready = dma_in("cmp_w_in0", cw[:, :, :], io["cmp_w"][0])
                yield from arrived("gates")
                needs(te, got["gates"], t_ident)
                for j in range(TT):
                    a = te.transpose(x_bank[:, j * 32:j * 32 + 24], made["gates"][:, j * P:(j + 1) * P], ident[0:24, 0:24])
                a = PE.did(a)
                yield
                needs(ve, a)
                t_gates = DVE.did(ve.tensor_copy(gates[:, :, :], x_bank[:, 0:P].rearrange("p (j c) -> p j c", j=TT)[:, :, 0:24]))
                blocks_free = None
                for which, name in enumerate(("k_cmp", "v_cmp")):
                    yield from arrived(name)
                    needs(ve, got[name], t_cols, blocks_free)
                    for half in range(2):
                        pe = cols[:, COLS["pe_v" if which else "pe_k"] + 16 * half:][:, 0:16]
                        b = DVE.did(ve.tensor_tensor(blk[:, 16 * half:16 * half + 16, 0:N_CMP],
                                                     made[name][:, 16 * half:16 * half + 496].rearrange("p (c s) -> p s c", s=16),
                                                     pe.unsqueeze(2).to_broadcast([P, 16, N_CMP]), ALU.add))
                    yield
                    needs(te, b, w_ready, t_gates, DVE.now())
                    for l in range(CMP_LEN):
                        a = te.matmul(x_bank[0:N_CMP, 256:256 + P], blk[:, l, 0:N_CMP], cw[:, l, :], start=(l == 0), stop=(l == CMP_LEN - 1))
                        if l % 8 == 7 and l < CMP_LEN - 1:
                            yield
                    blocks_free = a = PE.did(a)
                    if which == 0:
                        needs(gp, a)
                        w_ready = dma_in("cmp_w_in1", cw[:, :, :], io["cmp_w"][1], gp)
                    yield
                    needs(ve, a)
                    if which:
                        t_vc = DVE.did(ve.tensor_copy(vc[0:N_CMP, :], x_bank[0:N_CMP, 256:256 + P]))
                    else:
                        b = DVE.did(ve.tensor_copy(k_rows[0:N_CMP, :], x_bank[0:N_CMP, 256:256 + P]))
                        yield
                        needs(te, b)
                        a = PE.did(te.transpose(x_bank[:, 0:N_CMP], k_rows[0:N_CMP, :], ident[0:N_CMP, 0:N_CMP]))
                        yield
                        needs(ve, a)
                        b = DVE.did(ve.tensor_copy(k_cols[:, 0:N_CMP], x_bank[:, 0:N_CMP]))
                        yield
                        t_kc = rope(kc[:, 0:N_CMP], k_cols[:, 0:N_CMP], N_CMP, cos_c[:, 0:N_CMP], sin_c[:, 0:N_CMP],
                                    x_bank[:, 384:384 + N_CMP], b, None)
                for b, name in enumerate(("k_sel", "k_win")):
                    yield from arrived(name)
                    rope(keys[b][:, :], made[name][:, :], T, cos, sin, t_bank[0][:, :], got[name], DVE.now())
                    yield
                for b, name in enumerate(("v_sel", "v_win")):
                    yield from arrived(name)
                    to_natural(made[name], vals[b][:, :, :], s_bank[b][:, :], TT, [got[name], DVE.now()], None)
                    yield
                ends.extend((t_kc, t_vc))

            ends = []
            run_together((projections(), 1), (derived(), 1))
            t_kc, t_vc = ends
            barrier()

        q = [sb(st, f"nsa_q{s}", [P, T]) for s in range(2)]
        widths = (32, T, T)
        Pm = [[[sb(st, f"nsa_p{hh}{m}{b}", [P, w]) for b, w in enumerate(widths)] for m in range(2)] for hh in range(2)]
        PT = [[sb(st, f"nsa_pt{hh}{b}", [P, (w + P - 1) // P, P]) for b, w in enumerate(widths)] for hh in range(2)]
        small = [sb(st, f"nsa_small{hh}", [P, 12]) for hh in range(2)]
        o_banks = (o_bank, x_bank)

        q_ready = [None, None]

        def project_q(s, entry, late=False):
            b = used.n % 2
            t = yield from h_unit(b, late=late)
            needs(sc, t, *entry)
            a = lin_act[b].did(sc.activation(raw[:, :], lin[b][:, :], ACT.Copy))
            yield
            q_ready[s] = rope(q[s][:, :], raw[:, :], T, cos, sin, lin[b][:, :], a, entry, lin_dve[b])

        def heads(hh, pair, gate, entry):
            rows = slice(hh * DH, hh * DH + DH)
            S, Tb, sm = s_bank[hh], t_bank[hh], small[hh]
            s_free, t_free, pt_free, p_free = entry, entry, [entry] * 3, [entry, entry]
            before = None
            for m in range(2 * TT + 1):
                s, i = divmod(m, TT)
                s2, i2 = divmod(m - 1, TT)
                front = m < 2 * TT
                kw = (i + 1) * P
                ready = []
                for b, (key, w) in enumerate(((kc, N_CMP), (keys[0], kw), (keys[1], kw))):
                    if front:
                        needs(te, q_ready[s], s_free, t_kc)
                        a = PE.did(te.matmul(S[:, 0:w], q[s][rows, i * P:(i + 1) * P], key[rows, 0:w], start=True, stop=True))
                    if before:
                        was, w2 = Pm[hh][(m - 1) % 2][b], N_CMP if b == 0 else before[1]
                        needs(te, before[0][b], t_free)
                        for j in range(0, w2, P):
                            n = min(P, w2 - j)
                            c = te.transpose(Tb[0:n, j:j + P], was[:, j:j + n], ident[:, :])
                        p_free[(m - 1) % 2] = c = PE.did(c)
                        needs(sc, c, pt_free[b])
                        n = min(P, w2)
                        t_free = AC.did(sc.activation(PT[hh][b][0:n, 0:(w2 + P - 1) // P, :],
                                                      Tb[0:n, 0:max(w2, P)].rearrange("p (j q) -> p j q", q=P), ACT.Copy))
                    yield
                    if front:
                        needs(ve, a, t_cneg, t_neg, entry)
                        part = S[:, 0:w] if b == 0 else S[:, i * P:(i + 1) * P]
                        a = DVE.did(ve.tensor_tensor(part, part, cneg[:, i, 0:w] if b == 0 else neg[:, :], ALU.add))
                        yield
                        needs(sc, p_free[m % 2])
                        p, s_free = yield from softmax_rows(S[:, 0:w], Pm[hh][m % 2][b][:, 0:w], w, sm, b, SCALE, a, b == 0,
                                                 gates[:, i, gate(s, hh, b)])
                        ready.append(p)
                        yield
                    if before:
                        needs(te, t_free, t_vc)
                        out = o_banks[s2][rows, i2 * P:(i2 + 1) * P]
                        if b == 0:
                            c = te.matmul(out, vc[0:N_CMP, rows], PT[hh][0][0:N_CMP, 0, :], start=True, stop=False)
                        else:
                            for j in range(i2 + 1):
                                c = te.matmul(out, vals[b - 1][:, j, rows], PT[hh][b][:, j, :], start=False, stop=(b == 2 and j == i2))
                        pt_free[b] = PE.did(c)
                        if hh == 1 and b == 2 and i2 == TT - 1:
                            split(o_hi[:, pair(s2), :], o_lo[:, pair(s2), :], o_banks[s2][:, :], pt_free[2])
                        yield
                before = (ready, kw)

        table_set("exp_and_others")
        with pr.fori("nsa", 2) as i:
            entry = everything()
            q_ready[:] = [None, None]
            now(project_q(0, entry))

            def gate(s, hh, b):
                return bass.ds((i * 2 + s) * 3 + (12 * hh + b), 1)

            pair = lambda s: bass.ds(i * 2 + (4 + s), 1)
            run_together((heads(0, pair, gate, entry), 1), (heads(1, pair, gate, entry), 1), (project_q(1, entry, True), 1))

    def project_pair(bufs, s, entry, late):
        q, k, v, vT = bufs
        for dst in (q[s], k[s], vT):
            b = used.n % 2
            t = yield from h_unit(b, late=late)
            needs(sc, t, *entry)
            a = lin_act[b].did(sc.activation(dst[:, :], lin[b][:, :], ACT.Copy))
            yield
        return to_natural(vT, v[s][:, :, :], lin[b], TT, a, a, lin_act[b])

    def stick_phase(st, o_hi, o_lo):
        q = [sb(st, f"sb_q{s}", [P, T]) for s in range(2)]
        k = [sb(st, f"sb_k{s}", [P, T]) for s in range(2)]
        v = [sb(st, f"sb_v{s}", [P, TT, P]) for s in range(2)]
        vT = sb(st, "sb_vT", [P, T])
        strict = sb(st, "strict", [P, P])
        tri = sb(st, "tri", [P, P])
        t_strict = dma_in("strict_in", strict[:, :], tabs("strict_t", P))
        t_tri = dma_in("tri_in", tri[:, :], tabs("tri", P))
        work = [[sb(st, f"sb_{nm}{hh}", [P, T]) for nm in ("t", "ls0", "ls1", "lk0", "lk1")] for hh in range(2)]
        later = [sb(st, f"sb_later{hh}", [P, T]) for hh in range(2)]
        ready = [None, None]
        ada = ada_units(st)

        def project(s, entry, late=False):
            ready[s] = yield from project_pair((q, k, v, vT), s, entry, late)

        o_free = [None]

        def heads(hh, pair, entry):
            rows = slice(hh * DH, hh * DH + DH)
            tt, (ls_, lk_) = work[hh][0], (work[hh][1:3], work[hh][3:5])
            Z, A, rest = s_bank[hh], t_bank[hh], later[hh]
            z_free, tt_free, a_free, m2 = entry, entry, entry, entry
            ls_free, lk_free = [entry, entry], [entry, entry]
            before = None
            for m in range(2 * TT + 1):
                s, n = divmod(m, TT)
                front, par = m < 2 * TT, m % 2
                lo = T - (n + 1) * P
                w, ls, lk = slice(lo, T), ls_[par], lk_[par]
                if before:
                    s2, n2 = divmod(m - 1, TT)
                    lo2 = T - (n2 + 1) * P
                    w2, behind, old = slice(lo2, T), slice(lo2 + P, T), 1 - par
                    ls2, lk2, diag = ls_[old], lk_[old], slice(lo2, lo2 + P)
                if front:
                    needs(te, ready[s], z_free)
                    a = PE.did(te.matmul(Z[:, w], k[s][rows, lo:lo + P], q[s][rows, w], start=True, stop=True))
                if before:
                    needs(te, before, t_tri, a_free, m2)
                    b2 = te.matmul(A[:, w2], tri[:, :], lk2[:, w2], start=True, stop=(n2 == 0))
                    if n2:
                        b2 = te.matmul(A[:, behind], ones[:, :], rest[:, behind], start=False, stop=True)
                    b2 = PE.did(b2)
                    pr.needs_first(gp, before, b2)
                    if n2:
                        PO.did(gp.tensor_copy(rest[:, diag], lk2[:, diag]))
                        m2 = PO.did(gp.tensor_tensor(rest[:, behind], rest[:, behind], lk2[:, behind], ALU.add))
                    else:
                        m2 = PO.did(gp.tensor_copy(rest[:, w2], lk2[:, w2]))
                    lk_free[old] = [b2, m2]
                yield
                if front:
                    needs(sc, a, tt_free)
                    z_abs = b = AC.did(sc.activation(tt[:, w], Z[:, w], ACT.Abs, scale=SCALE))
                    needs(sc, b)
                    b = AC.did(sc.activation(tt[:, w], tt[:, w], ACT.Exp, scale=-1.0))
                if before:
                    needs(ve, b2)
                    a_free = c2 = DVE.did(ve.tensor_tensor(ls2[:, w2], A[:, w2], ls2[:, w2], ALU.add))
                yield
                if front:
                    needs(sc, b)
                    b = AC.did(sc.activation(tt[:, w], tt[:, w], ACT.Ln, bias=1.0))
                    needs(ve, z_abs, ls_free[par])
                    c = DVE.did(ve.tensor_scalar(ls[:, w], Z[:, w], SCALE, 0.0, ALU.mult, ALU.min))
                if before:
                    needs(sc, c2)
                    d2 = AC.did(sc.activation(ls2[:, w2], ls2[:, w2], ACT.Exp))
                yield
                if front:
                    needs(ve, b, c)
                    tt_free = c = DVE.did(ve.tensor_tensor(ls[:, w], ls[:, w], tt[:, w], ALU.subtract))
                    needs(ve, c, lk_free[par])
                    z_free = c = DVE.did(ve.scalar_tensor_tensor(lk[:, w], Z[:, w], -SCALE, ls[:, w], ALU.mult, ALU.add))
                if before:
                    needs(gp, d2, t_strict)
                    m3 = PO.did(gp.tensor_tensor(ls2[:, diag], ls2[:, diag], strict[:, :], ALU.mult))
                yield
                if front:
                    needs(gp, c, t_strict)
                    masked = PO.did(gp.tensor_tensor(lk[:, lo:lo + P], lk[:, lo:lo + P], strict[:, :], ALU.mult))
                if before:
                    needs(te, d2, m3, o_free[0])
                    j = TT - 1 - n2
                    a2 = te.matmul(o_bank[rows, diag], v[s2][:, j, rows], ls2[:, diag], start=(n2 == 0), stop=False)
                    if n2:
                        a2 = te.matmul(o_bank[rows, behind], v[s2][:, j, rows], ls2[:, behind], start=False, stop=(j == 0))
                    ls_free[old] = a2 = PE.did(a2)
                    if hh == 1 and j == 0:
                        o_free[0] = [split(o_hi[:, pair(s2), :], o_lo[:, pair(s2), :], o_bank[:, :], a2), AC.now()]
                yield
                before = front and masked

        table_set("natural_log_exp_and_others")
        with pr.fori("stick", 2) as i:
            entry = everything()
            ready[:], o_free[:] = [None, None], [entry]
            now(project(0, entry))
            pair = lambda s: bass.ds(i * 2 + s, 1)
            run_together((heads(0, pair, entry), 1), (heads(1, pair, entry), 1), (project(1, entry, True), 2), (ada(i, entry), 1))

    def ffn_phase(layer):
        with ExitStack() as st:
            g_hi = sb(st, f"g_hi{layer}", [P, FFH, T], F32R)
            g_lo = sb(st, f"g_lo{layer}", [P, FFH, T], F32R)
            a_in = sb(st, f"a_in{layer}", [P, T + 2])
            cv = [sb(st, f"cv{layer}{s}", [P, T]) for s in range(2)]
            gf = sb(st, f"gf{layer}", [P, T])
            needs(ve, t_cols)
            DVE.did(ve.memset(a_in[:, 0:2], 0.0))

            def hidden_tile(f, dst, then=KT):
                base = COLS["conv_w"] + layer * 3 * FFT
                tap = lambda n: cols[:, bass.ds(f + (base + n * FFT), 1)]
                bias = cols[:, bass.ds(f + (COLS["conv_b"] + layer * FFT), 1)]
                before = [DVE.now(), AC.now()]
                t = now(h_unit(0))
                needs(sc, t, *before)
                a = lin_act[0].did(sc.activation(a_in[:, 2:T + 2], lin[0][:, :], ACT.Copy))
                t2 = now(h_unit(1, then=then))
                needs(ve, a, *before)
                c = DVE.did(ve.tensor_scalar(cv[0][:, :], a_in[:, 0:T], tap(0), None, ALU.mult))
                needs(ve, c)
                c = DVE.did(ve.scalar_tensor_tensor(cv[1][:, :], a_in[:, 1:T + 1], tap(1), cv[0][:, :], ALU.mult, ALU.add))
                needs(ve, c)
                c = DVE.did(ve.scalar_tensor_tensor(cv[0][:, :], a_in[:, 2:T + 2], tap(2), cv[1][:, :], ALU.mult, ALU.add))
                needs(sc, c)
                a = AC.did(sc.activation(cv[1][:, :], cv[0][:, :], ACT.Silu, bias=bias))
                needs(ve, a, t2)
                c = lin_dve[1].did(ve.tensor_tensor(gf[:, :], lin[1][:, :], cv[1][:, :], ALU.mult))
                return split(g_hi[:, dst, :], g_lo[:, dst, :], gf[:, :], c)

            for half in range(2):
                table_set("silu_and_others")
                with pr.fori(f"ffn_in{layer}{half}", FFH - 1) as i:
                    hidden_tile(i + half * FFH, bass.ds(i, 1))
                tiles_in = DVE.now()
                last = hidden_tile(half * FFH + FFH - 1, FFH - 1, then=FFH)
                out_ready = [tiles_in] * (FFH - 1) + [last]
                if half:
                    clear_squares()
                with pr.fori(f"ffn_out{layer}{half}", KT // 2 - 1) as i:
                    out_units(i, g_hi, g_lo, blocks=FFH, thens=(FFH, FFH), squares=half == 1, ready=out_ready)
                out_units(KT // 2 - 1, g_hi, g_lo, blocks=FFH, thens=(FFH, KT), squares=half == 1, ready=out_ready)
                if half:
                    barrier()

    def odd_phase():
        with ExitStack() as st:
            o_hi = sb(st, "fo_hi", [P, KT, T], F32R)
            o_lo = sb(st, "fo_lo", [P, KT, T], F32R)
            with ExitStack() as s2:
                fox_phase(s2, o_hi, o_lo)
                barrier()
            out_proj("od_out", o_hi, o_lo)
            barrier()

    def fox_phase(st, o_hi, o_lo):
        q = [sb(st, f"fx_q{s}", [P, T]) for s in range(2)]
        k = [sb(st, f"fx_k{s}", [P, T]) for s in range(2)]
        v = [sb(st, f"fx_v{s}", [P, TT, P]) for s in range(2)]
        vT = sb(st, "fx_vT", [P, T])
        neg = sb(st, "fx_neg", [P, P])
        t_neg = dma_in("fx_neg_in", neg[:, :], tabs("causal_neg", P))
        cum = sb(st, "fx_cum", [P, T])
        u = sb(st, "fx_u", [P, T])
        z = sb(st, "fx_z", [P, T])
        Pm = [[sb(st, f"fx_p{hh}{b}", [P, T]) for b in range(2)] for hh in range(2)]
        PT = [[sb(st, f"fx_pt{hh}{b}", [P, TT, P]) for b in range(2)] for hh in range(2)]
        small = [sb(st, f"fx_small{hh}", [P, 8]) for hh in range(2)]
        row = [sb(st, f"fx_row{s}", [P, T]) for s in range(2)]
        fb = used.n % 2
        t = now(h_unit(fb))
        needs(sc, t, t_cols)
        needs(ve, t, t_cols)
        b_f = col("b_f")
        a = lin_act[fb].did(sc.activation(u[:, :], lin[fb][:, :], ACT.Abs, bias=b_f))
        needs(ve, a)
        needs(sc, a)
        a = AC.did(sc.activation(u[:, :], u[:, :], ACT.Exp, scale=-1.0))
        needs(sc, a)
        a = AC.did(sc.activation(u[:, :], u[:, :], ACT.Ln, bias=1.0))
        c = lin_dve[fb].did(ve.tensor_scalar(z[:, :], lin[fb][:, :], b_f, 0.0, ALU.add, ALU.min))
        needs(ve, a, c)
        c = DVE.did(ve.tensor_tensor(z[:, :], z[:, :], u[:, :], ALU.subtract))
        needs(ve, c)
        c = DVE.did(ve.memset(u[:, :], 1.0))
        needs(ve, c)
        c = DVE.did(ve.tensor_tensor_scan(cum[:, :], u[:, :], z[:, :], 0.0, ALU.mult, ALU.add))
        needs(ve, c)
        t_cum = DVE.did(ve.tensor_scalar(cum[:, :], cum[:, :], -1.0 / SCALE, None, ALU.mult))
        ready = [None, None]
        o_banks = (o_bank, x_bank)
        values_read = [None]

        def project(s, entry, late=False):
            ready[s] = yield from project_pair((q, k, v, vT), s, entry, late)

        def heads(hh, pair, pick, entry):
            rows = slice(hh * DH, hh * DH + DH)
            Tb, sm, S = t_bank[hh], small[hh], s_bank[hh]
            s_free, t_free, pt_free, p_free = entry, entry, [entry, entry], [entry, entry]
            before = None
            for m in range(2 * TT + 1):
                s, i = divmod(m, TT)
                front = m < 2 * TT
                kw = (i + 1) * P
                if front:
                    if i == 0:
                        needs(ve, t_cum, t_ident, entry)
                        c = DVE.did(ve.tensor_scalar(row[s][rows, :], cum[rows, :], pick(s, hh), None, ALU.mult))
                    needs(te, ready[s], c, s_free)
                    te.matmul(S[:, 0:kw], q[s][rows, i * P:(i + 1) * P], k[s][rows, 0:kw], start=True, stop=False)
                    a = PE.did(te.matmul(S[:, 0:kw], ones[rows, :], row[s][rows, 0:kw], start=False, stop=True))
                if before:
                    s2, i2 = divmod(m - 1, TT)
                    old, was, turned = (m - 1) % 2, Pm[hh][(m - 1) % 2], PT[hh][(m - 1) % 2]
                    needs(te, before, t_free)
                    for j in range(i2 + 1):
                        d = te.transpose(Tb[:, j * P:(j + 1) * P], was[:, j * P:(j + 1) * P], ident[:, :])
                    p_free[old] = d = PE.did(d)
                    needs(sc, d, pt_free[old])
                    t_free = AC.did(sc.activation(turned[:, 0:i2 + 1, :], Tb[:, 0:(i2 + 1) * P].rearrange("p (j q) -> p j q", q=P), ACT.Copy))
                yield
                if front:
                    needs(ve, a, t_neg)
                    diag = S[:, i * P:(i + 1) * P]
                    a = DVE.did(ve.tensor_tensor(diag, diag, neg[:, :], ALU.add))
                    needs(sc, p_free[m % 2])
                    yield
                    now_ready, s_free = yield from softmax_rows(S[:, 0:kw], Pm[hh][m % 2][:, 0:kw], kw, sm, m % 2, SCALE, a)
                    yield
                if before:
                    needs(te, t_free)
                    for j in range(i2 + 1):
                        a = te.matmul(o_banks[s2][rows, i2 * P:(i2 + 1) * P], v[s2][:, j, rows], turned[:, j, :], start=(j == 0), stop=(j == i2))
                    pt_free[old] = PE.did(a)
                    if hh == 1 and i2 == TT - 1:
                        values_read[0] = pt_free[old]
                        split(o_hi[:, pair(s2), :], o_lo[:, pair(s2), :], o_banks[s2][:, :], pt_free[old])
                    yield
                before = front and now_ready

        now(project(0, everything()))

        def two_pairs(i, more):
            entry = everything()
            ready[:] = [None, None]
            values_read[0] = None
            needs(te, entry)

            def feed():
                yield from project(1, entry, True)
                while more and values_read[0] is None:
                    yield
                if more:
                    yield from project(0, [values_read[0]], True)

            pick = lambda s, hh: ident[hh * DH:hh * DH + DH, bass.ds((i * 2 + s) * 2 + (hh + hh * DH), 1)]
            pair = lambda s: bass.ds(i * 2 + s, 1)
            run_together((heads(0, pair, pick, entry), 1), (heads(1, pair, pick, entry), 1), (feed(), 1))

        table_set("exp_and_others")
        with pr.fori("fox", 3) as i:
            two_pairs(i, True)
        two_pairs(3, False)

    NK = T + CTX
    NKT = NK // P

    def neighbour_phase(st, y_hi, y_lo, cx, t_cx):
        hc_hi = sb(st, "hc_hi", [P, KT, CTX], F32R)
        hc_lo = sb(st, "hc_lo", [P, KT, CTX], F32R)
        norm(cx, CTX, lambda k: scaled_g[:, 1, k:k + 1], lambda k: mod[:, k, 1:2], hc_hi, hc_lo, t_cx, False)
        barrier()
        q = [sb(st, f"na_q{s}", [P, T]) for s in range(2)]
        k = [sb(st, f"na_k{s}", [P, NK]) for s in range(2)]
        v = [sb(st, f"na_v{s}", [P, NKT, P]) for s in range(2)]
        vT = sb(st, "na_vT", [P, NK])
        bias = [sb(st, f"na_bias{s}", [P, 2 * 14, DH]) for s in range(2)]
        win = sb(st, "na_win", [P, DH])
        t_win = dma_in("win_in", win[:, :], tabs("win_neg", DH))
        Pm = [[sb(st, f"na_p{hh}{m}", [P, NK]) for m in range(2)] for hh in range(2)]
        PT = [sb(st, f"na_pt{hh}", [P, NKT, P]) for hh in range(2)]
        small = [sb(st, f"na_small{hh}", [P, 4]) for hh in range(2)]
        bias_in = [Counter(pr, f"na_bias_in{s}", 16) for s in range(2)]
        main = (slice(0, T), [(kk, h_hi[:, kk, :], h_lo[:, kk, :], h_ready[kk]) for kk in range(KT)])
        ready, b_ready = [None, None], [None, None]

        xb_read = [None]

        def project(s, pair, entry, late=False):
            needs(sc, *entry)
            t = bias_in[s].did(sc.dma_start(bias[s][:, :, :], io["bias"][pair].rearrange("a p (d c) -> p (a d) c", c=DH)))
            for n, dst in enumerate((q[s], k[s], vT)):
                b = used.n % 2
                xb = x_bank[:, (n - 1) * CTX:n * CTX] if n else None
                more = [(xb, [(kk, hc_hi[:, kk, :], hc_lo[:, kk, :]) for kk in range(KT)])] if n else []
                a = yield from unit(b, [main] + more, before=[*entry, xb_read[0]], late=late)
                needs(sc, a)
                a = lin_act[b].did(sc.activation(dst[:, 0:T], lin[b][:, :], ACT.Copy))
                if n:
                    xb_read[0] = a = AC.did(sc.activation(dst[:, T:NK], xb, ACT.Copy))
                yield
            a1 = to_natural(vT, v[s][:, 0:TT, :], lin[b], TT, [a, lin_act[b].now()], None, lin_act[b])
            xb_read[0] = a2 = to_natural(vT[:, T:NK], v[s][:, TT:NKT, :], x_bank, CTT, a, None)
            yield
            needs(ve, t, t_win)
            b_ready[s] = DVE.did(ve.tensor_tensor(bias[s][:, :, :], bias[s][:, :, :],
                                                  win[:, :].unsqueeze(1).to_broadcast([P, 28, DH]), ALU.add))
            ready[s] = [a1, a2]

        o_free = [None]

        def heads(hh, pair, entry):
            rows = slice(hh * DH, hh * DH + DH)
            S, Tb = s_bank[hh], t_bank[hh]
            free, pt_free, p_free = entry, entry, [entry, entry]
            before = None
            for m in range(2 * TT + 1):
                s, i = divmod(m, TT)
                s2, i2 = divmod(m - 1, TT)
                front, old = m < 2 * TT, (m - 1) % 2
                if front:
                    scores = Pm[hh][m % 2]
                    needs(te, ready[s], free)
                    lhs = q[s][rows, i * P:(i + 1) * P]
                    te.matmul(S[:, :], lhs, k[s][rows, 0:T], start=True, stop=True)
                    a = PE.did(te.matmul(Tb[:, 0:CTX], lhs, k[s][rows, T:NK], start=True, stop=True))
                    yield
                    needs(ve, a, b_ready[s], p_free[m % 2])
                    e0 = 14 * hh + 6 - 2 * i
                    c = DVE.did(ve.scalar_tensor_tensor(scores[:, 0:T], S[:, :], SCALE,
                                                        bias[s][:, e0:e0 + 8, :].rearrange("p d c -> p (d c)"), ALU.mult, ALU.add))
                    needs(sc, a, p_free[m % 2])
                    b = AC.did(sc.activation(scores[:, T:NK], Tb[:, 0:CTX], ACT.Copy, scale=SCALE))
                    free = [b, c]
                    yield
                if before:
                    was = Pm[hh][old]
                    needs(te, before, free)
                    for j in range(TT):
                        te.transpose(Tb[:, j * P:(j + 1) * P], was[:, j * P:(j + 1) * P], ident[:, :])
                    for j in range(CTT):
                        d = te.transpose(S[:, j * P:(j + 1) * P], was[:, T + j * P:T + (j + 1) * P], ident[:, :])
                    p_free[old] = d = PE.did(d)
                    needs(sc, d, pt_free)
                    AC.did(sc.activation(PT[hh][:, 0:TT, :], Tb[:, :].rearrange("p (j q) -> p j q", q=P), ACT.Copy))
                    free = turned = AC.did(sc.activation(PT[hh][:, TT:NKT, :], S[:, 0:CTX].rearrange("p (j q) -> p j q", q=P), ACT.Copy))
                    yield
                if front:
                    now_ready, _ = yield from softmax_rows(scores[:, :], scores[:, :], NK, small[hh], 0, 1.0, [b, c])
                    yield
                if before:
                    needs(te, turned, o_free[0])
                    for j in range(NKT):
                        a = te.matmul(o_bank[rows, i2 * P:(i2 + 1) * P], v[s2][:, j, rows], PT[hh][:, j, :], start=(j == 0), stop=(j == NKT - 1))
                    pt_free = PE.did(a)
                    if hh == 1 and i2 == TT - 1:
                        o_free[0] = [split(y_hi[:, pair(s2), :], y_lo[:, pair(s2), :], o_bank[:, :], pt_free), AC.now()]
                    yield
                before = front and now_ready

        table_set("exp_and_others")
        with pr.fori("neighbour", 2) as i:
            entry = everything()
            ready[:], b_ready[:], xb_read[:], o_free[:] = [None, None], [None, None], [None], [entry]
            now(project(0, bass.ds(i * 2, 1), entry))
            pair = lambda s: bass.ds(i * 2 + s, 1)
            run_together((heads(0, pair, entry), 1), (heads(1, pair, entry), 1),
                         (project(1, bass.ds(i * 2 + 1, 1), [*entry, *everything()], True), 2))
        barrier()

    CT = 4

    def gating_phase(st, y_hi, y_lo):
        gv = sb(st, "gv", [P, CT, T])
        u = sb(st, "gu", [P, CT, T])
        vn = sb(st, "vn", [P, TT, CT * P])
        wsT = sb(st, "wsT", [P, 8, P])
        bs = sb(st, "bs", [P, CT, P])
        t_ws = dma_in("ws_in", wsT[:, :, :], io["ws"])
        t_bs = dma_in("bs_in", bs[:, :, :], io["bs"])
        table_set("gelu_apprx_tanh_and_others")
        with pr.fori("gv", CT // 2) as i:
            for j in range(2):
                t = now(h_unit(j))
                needs(sc, t)
                lin_act[j].did(sc.activation(gv[:, bass.ds(i * 2 + j, 1), :], lin[j][:, :], ACT.Gelu_apprx_tanh))
        u_made = []

        def gelu_u():
            for k in range(CT):
                b = used.n % 2
                t = yield from h_unit(b, late=True)
                needs(sc, t)
                u_made.append(lin_act[b].did(sc.activation(u[:, k, :], lin[b][:, :], ACT.Gelu_apprx_tanh)))
                yield

        with ExitStack() as s2:
            mean = sb(s2, "ln_mean", [P, T])
            vn_made = []

            def layer_norm():
                s = column_sums(gv, CT, T, bank[2][:, :], False, [c.now() for c in lin_act])
                yield
                needs(ve, s)
                a = DVE.did(ve.tensor_scalar(mean[:, :], bank[2][:, :], 1.0 / (CT * P), None, ALU.mult))
                needs(ve, a)
                for k in range(CT):
                    a = DVE.did(ve.tensor_tensor(gv[:, k, :], gv[:, k, :], mean[:, :], ALU.subtract))
                    yield
                s = column_sums(gv, CT, T, bank[3][:, :], True, a)
                yield
                r = rstd_of(bank[3][:, :], T, CT * P, s)
                yield
                needs(ve, r)
                for k in range(CT):
                    a = DVE.did(ve.scalar_tensor_tensor(gv[:, k, :], gv[:, k, :], col("ln_g", k), ny[:, :], ALU.mult, ALU.mult))
                yield
                for n in range(TT):
                    b = t_bank[n % 2]
                    needs(te, a, vn_made[n - 2] if n >= 2 else None)
                    for k in range(CT):
                        c = te.transpose(b[:, k * P:(k + 1) * P], gv[:, k, n * P:(n + 1) * P], ident[:, :])
                    c = PE.did(c)
                    needs(sc, c)
                    vn_made.append(AC.did(sc.activation(vn[:, n, :], b[:, :], ACT.Copy)))
                    yield

            run_together((layer_norm(), 1), (gelu_u(), 1))
            needs(ve, u_made)
            r, t_vn = DVE.now(), vn_made
            tmp = [sb(s2, f"mix{k}", [P, T]) for k in range(2)]
            done = [None, None]
            for k in range(CT):
                b = s_bank[k % 2]
                needs(te, t_vn, t_ws, r, done[k % 2])
                for g2 in range(2):
                    for n in range(TT):
                        c = te.matmul(b[g2 * DH:(g2 + 1) * DH, n * P:(n + 1) * P], vn[:, n, k * P + g2 * DH:k * P + (g2 + 1) * DH],
                                      wsT[:, 2 * k + g2, :], start=True, stop=True)
                c = PE.did(c)
                needs(ve, c, t_bs, done[k % 2])
                c = DVE.did(ve.tensor_tensor(tmp[k % 2][:, :].rearrange("p (n q) -> p n q", n=TT), b[:, :].rearrange("p (n q) -> p n q", n=TT),
                                             bs[:, k, :].unsqueeze(1).to_broadcast([P, TT, P]), ALU.add))
                needs(ve, c)
                c = DVE.did(ve.tensor_tensor(tmp[k % 2][:, :], tmp[k % 2][:, :], u[:, k, :], ALU.mult))
                done[k % 2] = split(y_hi[:, k, :], y_lo[:, k, :], tmp[k % 2][:, :], c)
            barrier()

    def merge_phase(st, a_hi, a_lo, b_hi, b_lo, m_hi, m_lo):
        ga = sb(st, "ga", [P, T])
        gb = sb(st, "gb", [P, T])
        m = sb(st, "m", [P, T])
        table_set("sigmoid_and_others")
        with pr.fori("merge", KT // 2) as i:
            free = [DVE.now(), AC.now()]
            for j in range(2):
                for dst in (ga, gb):
                    b = used.n % 2
                    t = now(h_unit(b))
                    needs(sc, t, *free)
                    s = lin_act[b].did(sc.activation(dst[:, :], lin[b][:, :], ACT.Sigmoid))
                b = used.n % 2
                t = now(unit(b, [(slice(0, T), [(k, a_hi[:, k, :], a_lo[:, k, :]) for k in range(CT)]),
                                 (x_bank[:, :], [(CT + k, b_hi[:, k, :], b_lo[:, k, :]) for k in range(CT)])], before=free))
                needs(ve, t, s, lin_act[0].now(), lin_act[1].now())
                c = lin_dve[b].did(ve.tensor_tensor(ga[:, :], lin[b][:, :], ga[:, :], ALU.mult))
                d = DVE.did(ve.tensor_tensor(gb[:, :], x_bank[:, :], gb[:, :], ALU.mult))
                needs(ve, c, d, *free)
                d = DVE.did(ve.tensor_tensor(m[:, :], ga[:, :], gb[:, :], ALU.add))
                dst = bass.ds(i * 2 + j, 1)
                free = [split(m_hi[:, dst, :], m_lo[:, dst, :], m[:, :], d)]
        barrier()

    mod_flat = mod[:, :, :].rearrange("p a c -> p (a c)")
    H8 = 8
    K16 = 16
    G_TOK = 16
    G_BATCH = T // G_TOK
    AHEAD_COMBINE = 24 // TT
    u_dram = nc.dram_tensor("hidden_ahead", (AHEAD * H8, P, T), F32).ap()
    g_dram = nc.dram_tensor("expert_weights", (G_BATCH, P, HK, G_TOK), F32).ap()

    def top16(rows, ready):
        first = pr.needs_first
        first(ve, ready)
        got = [DVE.did(ve.max(vals[0], src)) for vals, index, src, work in rows]
        for n, (vals, index, src, work) in enumerate(rows):
            first(ve, got[n])
            DVE.did(ve.max_index(index[0], vals[0], src))
            got[n] = DVE.did(ve.match_replace(work, vals[0], src, -3e38))
        for n, (vals, index, src, work) in enumerate(rows):
            first(ve, got[n])
            got[n] = DVE.did(ve.max(vals[1], work))
        for n, (vals, index, src, work) in enumerate(rows):
            first(ve, got[n])
            last = DVE.did(ve.max_index(index[1], vals[1], work))
        return last

    def ahead_units(at, n, stage, spill):
        for k in range(n):
            b = used.n % 2
            t = yield from h_unit(b, late=True)
            needs(sc, t, spill[b].now())
            a = lin_act[b].did(sc.activation(stage[b][:, :], lin[b][:, :], ACT.Copy))
            needs(sc, a)
            spill[b].did(sc.dma_start(u_dram[bass.ds(at + k, 1), :, :].rearrange("a p t -> (a p) t"), stage[b][:, :]))
            yield

    def peer_phase():
        with ExitStack() as st:
            stage = [sb(st, f"u_stage{b}", [P, T]) for b in range(2)]
            spill = [Counter(pr, f"u_out{b}", 16) for b in range(2)]
            gT = sb(st, "gT", [P, T])
            iT = sb(st, "iT", [P, T])
            jT = sb(st, "jT", [P, T])
            with ExitStack() as s2:
                retrieve(s2, gT, iT, jT, stage, spill)
                barrier()
            with ExitStack() as s2:
                scatter(s2, gT, iT, jT, stage, spill)
                barrier()
            state["u_written"] = [c.now() for c in spill]
        with ExitStack() as st:
            experts(st)
            barrier()

    def retrieve(st, gT, iT, jT, stage, spill):
        keysT = sb(st, "keysT", [P, 16, P])
        t_keys = [spill[b].did(sc.dma_start(keysT[:, 8 * b:8 * b + 8, :], io["keys"][:, 8 * b:8 * b + 8, :])) for b in range(2)]
        iota16 = sb(st, "iota16", [P, K16])
        t_iota = dma_in("iota16_in", iota16[:, :], tabs("iota16", K16))
        KEYS_STEP = 4
        qT = [sb(st, f"pq{j}", [P, T]) for j in range(2)]
        s_sb = [sb(st, f"ps{j}", [P, TT, P]) for j in range(2)]
        work = [sb(st, f"pwork{j}", [P, 256]) for j in range(2)]
        vals = sb(st, "pvals", [P, TT, 16, K16])
        index = sb(st, "pindex", [P, TT, 16, K16], U32)
        now_v = sb(st, "pnow_v", [P, TT, KEYS_STEP, K16])
        now_i = sb(st, "pnow_i", [P, TT, KEYS_STEP, K16], U32)
        with pr.fori("keys", 16 // KEYS_STEP) as i:
            q_in, s_in, s_free = [None] * KEYS_STEP, [None] * KEYS_STEP, [None] * KEYS_STEP

            def query(j):
                b = j % 2
                t = yield from h_unit(b)
                needs(sc, t, PE.now())
                q_in[j] = lin_act[b].did(sc.activation(qT[b][:, :], lin[b][:, :], ACT.Copy))

            def match(j, before):
                b = j % 2
                needs(te, q_in[j], t_keys, before, s_in[j - 2] if j >= 2 else None)
                for n in range(TT):
                    a = te.matmul(t_bank[b][:, n * P:(n + 1) * P], qT[b][:, n * P:(n + 1) * P],
                                  keysT[:, bass.ds(i * KEYS_STEP + j, 1), :], start=True, stop=True)
                a = PE.did(a)
                needs(sc, a, before if j < 2 else s_free[j - 2])
                s_in[j] = AC.did(sc.activation(s_sb[b][:, :, :], t_bank[b][:, :].rearrange("p (n k) -> p n k", n=TT), ACT.Copy))
                yield
                for n0 in range(0, TT, 2):
                    two = [([now_v[:, n, j, 0:8], now_v[:, n, j, 8:16]], [now_i[:, n, j, 0:8], now_i[:, n, j, 8:16]],
                            s_sb[b][:, n, :], work[n % 2][:, 0:P]) for n in (n0, n0 + 1)]
                    s_free[j] = top16(two, [s_in[j], DVE.now()])
                    yield

            start = [AC.now(), DVE.now()]
            for j in range(KEYS_STEP):
                if j:
                    run_together((query(j), 1), (match(j - 1, start), 1))
                else:
                    now(query(j))
            now(match(KEYS_STEP - 1, start))
            needs(ve, DVE.now())
            DVE.did(ve.tensor_copy(vals[:, :, bass.ds(i * KEYS_STEP, KEYS_STEP), :], now_v[:, :, :, :]))
            DVE.did(ve.tensor_copy(index[:, :, bass.ds(i * KEYS_STEP, KEYS_STEP), :], now_i[:, :, :, :]))
        barrier()
        cand = sb(st, "cand", [P, H8, K16, K16])
        oh = sb(st, "oh", [P, H8, K16, K16])
        best = sb(st, "best", [P, H8, K16])
        pos = sb(st, "pos", [P, H8, K16], U32)
        part = sb(st, "part", [P, H8, K16], U32)
        partf = sb(st, "partf", [P, H8, K16])
        idxf = sb(st, "idxf", [P, H8, 2, K16])
        rs = sb(st, "prs", [P, H8])
        res = sb(st, "pres", [P, 3, P])
        table_set("exp_and_others")

        def combine(i):
            needs(ve, AC.now(), PE.now(), DVE.now(), t_iota)
            mine = bass.ds(i, 1)
            v4 = vals[:, mine, :, :].rearrange("p a (h c) k -> p (a h) c k", c=2)
            first = v4[:, :, 0, :].unsqueeze(3).to_broadcast([P, H8, K16, K16])
            second = v4[:, :, 1, :].unsqueeze(2).to_broadcast([P, H8, K16, K16])
            a = DVE.did(ve.tensor_tensor(cand[:, :, :, :], first, second, ALU.add))
            DVE.did(ve.tensor_copy(idxf[:, :, :, :].rearrange("p h c k -> p (h c) k"), index[:, mine, :, :].rearrange("p a c k -> p (a c) k")))
            for h0 in range(0, H8, 2):
                two = [([best[:, h, 0:8], best[:, h, 8:16]], [pos[:, h, 0:8], pos[:, h, 8:16]],
                        cand[:, h, :, :].rearrange("p a b -> p (a b)"), work[h % 2][:, :]) for h in (h0, h0 + 1)]
                a = top16(two, [a, DVE.now()])
                yield
            needs(ve, a)
            g3 = res[:, 0, :].rearrange("p (h k) -> p h k", h=H8)
            c = DVE.did(ve.tensor_tensor(g3, best[:, :, :], best[:, :, 0:1].to_broadcast([P, H8, K16]), ALU.subtract))
            needs(sc, c)
            b = AC.did(sc.activation(res[:, 0, :], res[:, 0, :], ACT.Exp))
            needs(ve, b)
            c = DVE.did(ve.tensor_reduce(rs[:, :], g3, AX.X, ALU.add))
            needs(ve, c)
            c = DVE.did(ve.reciprocal(rs[:, :], rs[:, :]))
            needs(ve, c)
            c = DVE.did(ve.tensor_tensor(g3, g3, rs[:, :].unsqueeze(2).to_broadcast([P, H8, K16]), ALU.mult))
            yield
            for half in range(2):
                if half == 0:
                    c = DVE.did(ve.tensor_scalar(part[:, :, :], pos[:, :, :], 4, None, ALU.logical_shift_right))
                else:
                    c = DVE.did(ve.tensor_scalar(part[:, :, :], pos[:, :, :], 15, None, ALU.bitwise_and))
                needs(ve, c)
                c = DVE.did(ve.tensor_copy(partf[:, :, :], part[:, :, :]))
                needs(ve, c)
                o3 = oh[:, :, :, :].rearrange("p h k a -> p (h k) a")
                c = DVE.did(ve.tensor_tensor(o3, partf[:, :, :].rearrange("p h k -> p (h k)").unsqueeze(2).to_broadcast([P, HK, K16]),
                                             iota16[:, :].unsqueeze(1).to_broadcast([P, HK, K16]), ALU.is_equal))
                needs(ve, c)
                yield
                c = DVE.did(ve.tensor_tensor(oh[:, :, :, :], oh[:, :, :, :],
                                             idxf[:, :, half, :].unsqueeze(2).to_broadcast([P, H8, K16, K16]), ALU.mult))
                needs(ve, c)
                yield
                c = DVE.did(ve.tensor_reduce(res[:, 1 + half, :], o3, AX.X, ALU.add))
                needs(ve, c)
                yield
            needs(te, c)
            for n in range(3):
                a = te.transpose(t_bank[0][:, n * P:(n + 1) * P], res[:, n, :], ident[:, :])
            a = PE.did(a)
            needs(sc, a)
            for n, dst in enumerate((gT, iT, jT)):
                AC.did(sc.activation(dst[:, bass.ds(i * P, P)], t_bank[0][:, n * P:(n + 1) * P], ACT.Copy))

        with pr.fori("combine", TT) as i:
            run_together((combine(i), 1), (ahead_units(i * AHEAD_COMBINE, AHEAD_COMBINE, stage, spill), 3))

    def scatter(st, gT, iT, jT, stage, spill):
        iota = sb(st, "iota", [P, P])
        A = [sb(st, f"oneA{b}", [P, 4, P]) for b in range(8)]
        B = [sb(st, f"oneB{b}", [P, 4, P]) for b in range(8)]
        j_now = sb(st, "j_now", [P, 4 * G_TOK])
        G = [sb(st, f"G{b}", [P, HK, G_TOK]) for b in range(2)]
        banks = s_bank + t_bank
        out = [Counter(pr, f"G_dma{b}", 16) for b in range(2)]
        t_iota = [out[b].did(sc.dma_start(iota[:, b * DH:(b + 1) * DH], tabs("iota", P)[:, b * DH:(b + 1) * DH])) for b in range(2)]
        needs(ve, t_iota)
        needs(gp, t_iota)

        def batches(i):
            pe_t = [PE.now(7 - b) for b in range(8)]
            act_t = [AC.now(3 - b) for b in range(4)]
            pr.needs_first(gp, PO.now())
            b = PO.did(gp.tensor_copy(j_now[:, :], jT[:, bass.ds(i * 4 * G_TOK, 4 * G_TOK)]))
            pr.needs_first(gp, b)
            for quarter in range(4):
                half = quarter % 2
                needs(sc, out[half].now())
                for grp in range(4):
                    k = quarter * G_TOK + grp * 4
                    buf = half * 4 + grp
                    if grp % 2:
                        pr.needs_first(gp, pe_t[buf])
                        for n in range(4):
                            b = PO.did(gp.tensor_scalar(B[buf][:, n, :], iota[:, :], j_now[:, k + n:k + n + 1], None, ALU.is_equal))
                        needs(ve, pe_t[buf])
                    else:
                        needs(ve, pe_t[buf])
                        four = jT[:, bass.ds(i * 4 * G_TOK + k, 4)]
                        b = DVE.did(ve.tensor_tensor(B[buf][:, :, :], iota[:, :].unsqueeze(1).to_broadcast([P, 4, P]),
                                                     four.unsqueeze(2).to_broadcast([P, 4, P]), ALU.is_equal))
                    for n in range(4):
                        tok = bass.ds(i * 4 * G_TOK + (k + n), 1)
                        a = DVE.did(ve.tensor_scalar(A[buf][:, n, :], iota[:, :], iT[:, tok], gT[:, tok], ALU.is_equal, ALU.mult))
                    needs(te, a, b, act_t[grp])
                    for n in range(4):
                        c = te.matmul(banks[grp][:, n * P:(n + 1) * P], B[buf][:, n, :], A[buf][:, n, :], start=True, stop=True)
                    pe_t[buf] = PE.did(c)
                    needs(sc, pe_t[buf])
                    act_t[grp] = AC.did(sc.activation(G[half][:, :, grp * 4:grp * 4 + 4],
                                                      banks[grp][:, :].rearrange("p (t i) -> p i t", t=4), ACT.Copy))
                    yield
                needs(sc, act_t[3])
                out[half].did(sc.dma_start(g_dram[bass.ds(i * 4 + quarter, 1), :, :, :].rearrange("a p i t -> (a p) i t"), G[half][:, :, :]))

        passes = G_BATCH // 4
        units = AHEAD * H8 // passes - TT * AHEAD_COMBINE // passes
        with pr.fori("scatter", passes) as i:
            run_together((batches(i), 3), (ahead_units(i * units + TT * AHEAD_COMBINE, units, stage, spill), 2))
        state["g_written"] = [c.now() for c in out]

    def experts(st):
        Gin = sb(st, "Gin", [P, G_BATCH, H8, G_TOK])
        af = [sb(st, f"af{j}", [P, T]) for j in range(2)]
        e_hi = sb(st, "e_hi", [P, KT, T], F32R)
        e_lo = sb(st, "e_lo", [P, KT, T], F32R)
        g_in = Counter(pr, "G_in", 16)
        needs(gp, state["g_written"])

        half_in = [Counter(pr, f"ahead_in{s}", 16) for s in range(2)]
        halves = [sb(st, f"ahead{s}", [P, KT // 2, T]) for s in range(2)]
        af_free = [None, None]
        e_parts = ((e_hi, e_lo), (h_hi, h_lo))

        def fetch_g(i, free):
            needs(gp, free)
            g_in.did(gp.dma_start(Gin[:, :, :, :].rearrange("p b i t -> p b (i t)"),
                                  g_dram[:, :, bass.ds(i * H8, H8) if not isinstance(i, int) else slice(i * H8, (i + 1) * H8), :]
                                  .rearrange("b p i t -> p b (i t)")))

        def fetch_ahead(i, half, free):
            needs(gp, free)
            at = i * KT + half * (KT // 2)
            src = u_dram[at:at + KT // 2, :, :] if isinstance(i, int) else u_dram[bass.ds(at, KT // 2), :, :]
            half_in[half].did(gp.dma_start(halves[half][:, :, :], src.rearrange("u p t -> p u t")))

        def hidden(j, src, ready, reader, parts, t_g):
            b = j % 2
            needs(sc, ready, af_free[b])
            a = reader.did(sc.activation(af[b][:, :], src, ACT.Gelu_apprx_tanh))
            needs(ve, a, t_g)
            c = DVE.did(ve.tensor_tensor(af[b][:, :].rearrange("p (b t) -> p b t", t=G_TOK),
                                         af[b][:, :].rearrange("p (b t) -> p b t", t=G_TOK), Gin[:, :, j, :], ALU.mult))
            af_free[b] = split(parts[0][:, j, :], parts[1][:, j, :], af[b][:, :], c)
            return af_free[b], c, a

        def v_units(parts, ready, squares=False, meanwhile=None):
            for n in range(KT):
                b = n % 2
                t = now(unit(b, [(slice(0, T), [(k, parts[0][:, k, :], parts[1][:, k, :], ready[k]) for k in range(KT)])]))
                if meanwhile:
                    for j in ((0, 1), (2, 3), (4,), (5,), (6,), (7,), (), ())[n]:
                        meanwhile(j)
                needs(ve, t)
                a = lin_dve[b].did(ve.scalar_tensor_tensor(x[:, n, :], lin[b][:, :], mod[:, 5 * KT + n, 0:1], x[:, n, :], ALU.mult, ALU.add))
                if squares:
                    add_squares(n, x[:, n, :], a)

        def whole_group():
            t_g = g_in.now()
            af_free[:] = [DVE.now(), DVE.now()]
            ready = []
            for j in range(KT):
                t = now(h_unit(j % 2))
                r, c, _ = hidden(j, lin[j % 2][:, :], t, lin_act[j % 2], e_parts[0], t_g)
                ready.append(r)
            return ready, c

        def fill(parts, busy, then):
            t_g, t_h = g_in.now(), [c.now() for c in half_in]
            ready = []

            def tile(j):
                half, at = divmod(j, KT // 2)
                needs(sc, busy)
                r, c, a = hidden(j, halves[half][:, at, :], t_h[half], AC, parts, t_g)
                ready.append(r)
                if then is not None and at == KT // 2 - 1:
                    fetch_ahead(then, half, a)
                    if half:
                        fetch_g(then, c)
            return tile, ready

        needs(gp, state["u_written"])
        fetch_g(AHEAD, everything())
        for half in range(2):
            fetch_ahead(0, half, None)
        table_set("gelu_apprx_tanh_and_others")
        with pr.fori("experts", PEER_GROUPS - AHEAD - 1) as i:
            ready, c = whole_group()
            fetch_g(i + (AHEAD + 1), c)
            v_units(e_parts[0], ready)
        ready, c = whole_group()
        fetch_g(0, c)
        tile, filled = fill(e_parts[1], used.now(), 1)
        v_units(e_parts[0], ready, meanwhile=tile)
        with pr.fori("experts_ahead", (AHEAD - 1) // 2) as i:
            for s in range(2):
                ready = filled if s else [DVE.now()] * KT
                if not s:
                    af_free[:] = [DVE.now(), DVE.now()]
                tile, filled = fill(e_parts[s], used.now(), i + 3 if s else i * 2 + 2)
                v_units(e_parts[1 - s], ready, meanwhile=tile)
        clear_squares()
        v_units(e_parts[1], [DVE.now()] * KT, squares=True)
        needs(gp, g_in.now(), [c.now() for c in half_in])
        needs(sc, g_in.now(), [c.now() for c in half_in])

    state = {}
    y_out = Counter(pr, "y_out", 16)

    def gain_of(name, off=0):
        return lambda k: col(name, off + k)

    for b in range(2):
        lin_dve[b].did(ve.memset(scaled_g[:, b, :], 0.0))
    split_weights()
    norm(x, T, gain_of("attn_norm"), None, h_hi, h_lo, t_x, False)
    even_phase()
    norm(x, T, gain_of("ffn_norm"), None, h_hi, h_lo)
    ffn_phase(0)
    norm(x, T, gain_of("attn_norm", KT), None, h_hi, h_lo)
    odd_phase()
    norm(x, T, gain_of("ffn_norm", KT), None, h_hi, h_lo)
    ffn_phase(1)
    with ExitStack() as st:
        ya = [sb(st, f"ya{p}", [P, CT, T], F32R) for p in range(2)]
        yb = [sb(st, f"yb{p}", [P, CT, T], F32R) for p in range(2)]
        cx = sb(st, "ctx_x", [P, KT, CTX])
        t_cx = dma_in("ctx_in", cx[:, :, :], io["ctx"])
        norm_plain(gain_of("final_norm"), True)
        norm(x, T, lambda k: scaled_g[:, 0, k:k + 1], lambda k: mod[:, k, 0:1], h_hi, h_lo)
        with ExitStack() as s2:
            neighbour_phase(s2, *ya, cx, t_cx)
        with ExitStack() as s2:
            gating_phase(s2, *yb)
        with ExitStack() as s2:
            m_hi, m_lo = (sb(s2, f"m_part{p}", [P, KT, T], F32R) for p in range(2))
            merge_phase(s2, *ya, *yb, m_hi, m_lo)
            out_proj("out2", m_hi, m_lo, lambda n: mod_flat[:, bass.ds(n * 2 + 4 * KT, 1)])
            barrier()
    norm(x, T, lambda k: scaled_g[:, 2, k:k + 1], lambda k: mod[:, 3 * KT + k, 0:1], h_hi, h_lo)
    peer_phase()
    norm_plain(gain_of("final_g"), False)
    needs(sc, everything(), y_out.now())
    assert used.n == n_units == lo_done.n, (used.n, n_units, lo_done.n)
    pr.stack.close()
    return pr.found


def units_of(w, blocks=KT):
    k, n = w.shape
    return w.reshape(blocks, P, n // P, P).transpose(2, 1, 0, 3).reshape(n // P, P, blocks * P)


def padded(w, n=P):
    out = np.zeros((w.shape[0], n), w.dtype)
    out[:, :w.shape[1]] = w
    return out


def by_tile(v):
    return v.reshape(-1, P).T


def tables():
    t = np.zeros((P, N_TABS), np.float32)

    def put(name, a):
        t[:a.shape[0], TABS[name]:TABS[name] + a.shape[1]] = a

    inv = np.float32(500000.0) ** (-(np.arange(8, dtype=np.float32) * np.float32(2.0) / np.float32(16)))
    for c, s, pos in (("cos", "sin", np.arange(T)), ("cos_cmp", "sin_cmp", np.arange(N_CMP) * 16 + CMP_LEN - 1)):
        ang = (pos.astype(np.float32)[None, :] * inv[:, None]).astype(np.float32).astype(np.float64)
        cos, sin = np.ones((P, len(pos))), np.zeros((P, len(pos)))
        for base in (0, DH):
            for half in (0, 8):
                cos[base + half:base + half + 8] = np.cos(ang)
                sin[base + half:base + half + 8] = np.sin(ang)
        put(c, cos.astype(np.float32))
        put(s, sin.astype(np.float32))
    perm = np.zeros((P, P), np.float32)
    for base in (0, DH):
        for d in range(8):
            perm[base + 8 + d, base + d] = -1.0
            perm[base + d, base + 8 + d] = 1.0
    put("perm", perm)
    put("ident", np.eye(P, dtype=np.float32))
    r = np.arange(P)
    put("causal_neg", np.where(r[None, :] <= r[:, None], 0.0, NEG).astype(np.float32))
    put("strict_t", (r[:, None] < r[None, :]).astype(np.float32))
    put("tri", (r[:, None] > r[None, :]).astype(np.float32))
    c = np.arange(DH)
    start = np.clip(c - 8, 0, DH - 16)
    win = np.where((c[None, :] >= start[:, None]) & (c[None, :] < start[:, None] + 16), 0.0, NEG).astype(np.float32)
    put("win_neg", np.concatenate([win, win]))
    tok = np.arange(T).reshape(TT, P)
    end = np.arange(32) * 16 + CMP_LEN - 1
    cm = np.where(end[None, None, :] <= tok[:, :, None], 0.0, NEG).astype(np.float32)
    put("cmp_neg", cm.transpose(1, 0, 2).reshape(P, TT * 32))
    put("iota", np.broadcast_to(np.arange(P, dtype=np.float32), (P, P)))
    put("iota16", np.broadcast_to(np.arange(16, dtype=np.float32), (P, 16)))
    return t


def layout(a):
    ev = a["ev_w_in"][0]
    off = np.cumsum([0, 512, 512, 512, 512, 128, 128, 128, 128, 128, 128, 24])
    seg = [ev[:, off[n]:off[n + 1]] for n in range(11)]
    sq, sk, sv, nq, kc, vc, ksl, vsl, kwn, vwn, gate = seg
    head = lambda w, h: w[:, h * DH:(h + 1) * DH]
    pair = lambda w, p: w[:, p * P:(p + 1) * P]
    small = [padded(gate), kc, vc, ksl, kwn, vsl, vwn]
    small += [np.concatenate([head(nq, p), head(nq, p + 4)], 1) for p in range(4)]
    small += [pair(w, p) for p in range(4) for w in (sq, sk, sv)]
    u8 = [units_of(w) for w in small]
    wo = a["ev_w_out"][0]
    rows = [wo[0:512]] + [wo[512 + h * DH:512 + (h + 1) * DH] for p in range(4) for h in (p, p + 4)]
    u8.append(units_of(np.concatenate(rows)))
    u11 = []
    for layer in range(2):
        if layer == 1:
            od = a["od_w_in"][0]
            f = od[:, 3072:3088]
            u8.append(units_of(np.concatenate([padded(f, DH), padded(f, DH)], 1)))
            u8 += [units_of(pair(od[:, 1024 * n:1024 * (n + 1)], p)) for p in range(8) for n in range(3)]
            u8.append(units_of(a["od_w_out"][0]))
        w = units_of(a["ffn_w_in"][layer]).reshape(2, FFT, P, D)
        u8.append(w.transpose(1, 0, 2, 3).reshape(2 * FFT, P, D))
        w = a["ffn_w_out"][layer]
        u11 += [units_of(w[h * FFH * P:(h + 1) * FFH * P], FFH) for h in range(2)]
    w = a["w_in_2"][0]
    u8 += [units_of(pair(w[:, 512 * n:512 * (n + 1)], p)) for p in range(4) for n in range(3)]
    u8 += [units_of(w[:, 2048:2560]), units_of(w[:, 1536:2048])]
    pab = np.concatenate([a["w_proj_a_2"][0], a["w_proj_b_2"][0]])
    three = np.stack([units_of(w[:, 2560:3584]), units_of(w[:, 3584:4608]), units_of(pab)], 1)
    u8.append(three.reshape(24, P, D))
    u8.append(units_of(a["w_out_2"][0]))
    u8.append(units_of(a["peer_wq_2"][0]))
    U = a["peer_u_2"][0].reshape(PEER_GROUPS, 8, P, KT, P).transpose(0, 1, 4, 3, 2).reshape(PEER_GROUPS, 8, P, D)
    V = a["peer_v_2"][0].reshape(PEER_GROUPS, 8, P, KT, P).transpose(0, 3, 2, 1, 4).reshape(PEER_GROUPS, 8, P, D)
    u8 += [m.reshape(-1, P, D) for m in (U[:AHEAD], np.concatenate([U[AHEAD:], V[AHEAD:]], 1), V[:AHEAD])]
    ada = a["ada_w_2"][0].reshape(KT, P, -1, 256).transpose(2, 1, 0, 3)
    out = {"ada_w": ada, "w8": np.concatenate(u8), "w11": np.concatenate(u11), "tabs": tables()}
    to_tiles = lambda m: m.T.reshape(KT, P, -1).transpose(1, 0, 2)
    out["x"] = to_tiles(a["x"][0])
    out["ctx"] = to_tiles(a["ctx_2"][0])
    cols = np.zeros((P, N_COLS), np.float32)

    def put(name, m):
        cols[:, COLS[name]:COLS[name] + m.shape[1]] = m

    for name, key in (("attn_norm", "attn_norm"), ("ffn_norm", "ffn_norm"), ("final_norm", "final_norm"), ("norm1", "norm1_g_2"),
                      ("norm2", "norm2_g_2"), ("final_g", "final_g_2"), ("conv_w", "ffn_conv_w"), ("conv_b", "ffn_conv_b"),
                      ("ada_b", "ada_b_2"), ("ln_g", "gm_ln_g_2")):
        put(name, by_tile(np.ascontiguousarray(a[key]).reshape(-1)))
    bf = np.zeros((P, 1), np.float32)
    bf[0:16, 0] = bf[DH:DH + 16, 0] = a["od_b_f"][0]
    put("b_f", bf)
    put("c", np.stack([by_tile(a["c_2"].reshape(-1)), by_tile(a["c_ctx_2"])], 2).reshape(P, 16))
    for name, key in (("pe_k", "ev_cmp_pos_k"), ("pe_v", "ev_cmp_pos_v")):
        put(name, np.concatenate([a[key][0].T, a[key][0].T]))
    out["cols"] = cols
    cw = np.zeros((2, P, CMP_LEN, P), np.float32)
    for n, key in enumerate(("ev_cmp_w_k", "ev_cmp_w_v")):
        w = a[key][0].reshape(CMP_LEN, DH, DH).transpose(1, 0, 2)
        cw[n, 0:DH, :, 0:DH] = w
        cw[n, DH:, :, DH:] = w
    out["cmp_w"] = cw
    rpb = a["na_rpb_2"][0]
    c = np.arange(DH)
    dc = np.clip(c[None, :] - c[:, None] + 15, 0, 30)
    e = np.arange(1, 15)
    b = np.stack([rpb[:, (e - r)[:, None, None], dc[None]] for r in range(2)], 1)
    out["bias"] = b.transpose(0, 1, 3, 2, 4).reshape(4, 2, P, 14, DH).transpose(0, 2, 1, 3, 4).reshape(4, P, 28 * DH)
    out["ws"] = a["gm_ws_2"][0].transpose(2, 0, 1)
    out["bs"] = np.repeat(a["gm_bs_2"][0].reshape(4, 2, 1, P), DH, axis=2).reshape(4, P, P).transpose(1, 0, 2)
    out["keys"] = a["peer_keys_2"][0].reshape(16, P, P).transpose(2, 0, 1)
    return {k: np.ascontiguousarray(v) for k, v in out.items()}


def build(nc, shapes, deltas):
    io = {n: nc.dram_tensor(f"in_{n}", v, F32, kind="ExternalInput").ap() for n, v in shapes.items()}
    io["out"] = nc.dram_tensor("out_y", (P, KT, T), F32, kind="ExternalOutput").ap()
    return program(nc, io, deltas)


def kernel(**inputs):
    from concourse import bacc
    from concourse.bass_utils import run_bass_kernel_spmd
    arrays = layout({k: np.asarray(v) for k, v in inputs.items()})
    shapes = {k: v.shape for k, v in arrays.items()}
    deltas = {}
    for _ in range(2):
        nc = bacc.Bacc("TRN2", target_bir_lowering=False, num_devices=1)
        deltas = build(nc, shapes, deltas)
    r = run_bass_kernel_spmd(nc, [{f"in_{k}": v for k, v in arrays.items()}], core_ids=[0])
    y = r.results[0]["out_y"]
    return np.ascontiguousarray(y.transpose(2, 1, 0).reshape(1, T, D))
```
